# Optimizing a Trainium2 kernel written in Bass

```python
import math
import jax, jax.numpy as jnp
from jax import lax
import numpy as np

D_MODEL = 1024
BATCH = 1
SEQ = 512
DEPTH = 1

ATTN_WINDOWS = (128, 512, 2048)
ATTN_DILATIONS = (1, 4, 16)
N_GROUPS = len(ATTN_WINDOWS)
ATTN_HEAD_DIM = 64
ATTN_HEADS_PER_GROUP = D_MODEL // 128
N_ATTN_HEADS = N_GROUPS * ATTN_HEADS_PER_GROUP
ATTN_OUT_WIDTH = ATTN_HEADS_PER_GROUP * ATTN_HEAD_DIM
ATTN_QKV_WIDTH = N_GROUPS * 3 * ATTN_HEADS_PER_GROUP * ATTN_HEAD_DIM
ATTN_BLOCK = 128
NEG_INF = -1e30
NUM_BUCKETS = 32
MAX_EXACT = NUM_BUCKETS // 2
MAX_DISTANCE = 2048
HGRN_HEADS = D_MODEL // 256
HGRN_DK = 128
HGRN_DV = 128
HGRN_WIDTH = HGRN_HEADS * HGRN_DK
HGRN_CHUNK = 32
GATE_WIDTH = 2 * D_MODEL
IN_WIDTH = ATTN_QKV_WIDTH + 4 * HGRN_WIDTH + GATE_WIDTH
D_FF = ((8 * D_MODEL // 3 + 127) // 128) * 128
CONV_WIDTH = 3
NORM_EPS = 1e-6

kernel_name = "hybrid_dilated_attn_hgrn2_convffn"

def rms_norm(x, w):
    xf = x.astype(jnp.float32)
    y = xf * lax.rsqrt(jnp.mean(xf * xf, axis=-1, keepdims=True) + NORM_EPS)
    return (y * w.astype(jnp.float32)).astype(x.dtype)

def t5_bucket(dist):
    n = jnp.maximum(dist, 0)
    nf = jnp.maximum(n, 1).astype(jnp.float32)
    large = MAX_EXACT + (jnp.log(nf / MAX_EXACT) / math.log(MAX_DISTANCE / MAX_EXACT)
                         * (NUM_BUCKETS - MAX_EXACT)).astype(jnp.int32)
    large = jnp.minimum(large, NUM_BUCKETS - 1)
    return jnp.where(n < MAX_EXACT, n, large)

def dilated_window_attention(q, k, v, bias_table, dilation, window):
    Bn, S, H, hd = q.shape
    blk = ATTN_BLOCK
    span = dilation * blk
    Sp = -(-S // span) * span
    pad = ((0, 0), (0, Sp - S), (0, 0), (0, 0))
    q, k, v = jnp.pad(q, pad), jnp.pad(k, pad), jnp.pad(v, pad)
    U = Sp // dilation
    NB = U // blk

    def to_sub(t):
        return t.reshape(Bn, U, dilation, H, hd).transpose(0, 2, 3, 1, 4)

    def band(t):
        ts = to_sub(t)
        prev = jnp.pad(ts, ((0, 0), (0, 0), (0, 0), (blk, 0), (0, 0)))[:, :, :, :U]
        return jnp.concatenate([prev.reshape(Bn, dilation, H, NB, blk, hd),
                                ts.reshape(Bn, dilation, H, NB, blk, hd)], axis=-2)

    qs = to_sub(q).reshape(Bn, dilation, H, NB, blk, hd)
    kb, vb = band(k), band(v)
    s = jnp.einsum('bdhnqe,bdhnke->bdhnqk', qs, kb).astype(jnp.float32) * (hd ** -0.5)

    rel = jnp.arange(blk)[:, None] + blk - jnp.arange(2 * blk)[None, :]
    in_win = (rel >= 0) & (rel <= window // dilation)
    key_ok = (jnp.arange(NB)[:, None] * blk - blk + jnp.arange(2 * blk)[None, :]) >= 0
    mask = in_win[None] & key_ok[:, None, :]
    bias = bias_table[t5_bucket(rel * dilation)].astype(jnp.float32)
    s = s + bias.transpose(2, 0, 1)[:, None]
    s = jnp.where(mask, s, NEG_INF)

    m = jnp.max(s, axis=-1, keepdims=True)
    p = jnp.exp(s - m)
    l = jnp.sum(p, axis=-1, keepdims=True)
    o = jnp.einsum('bdhnqk,bdhnke->bdhnqe', p.astype(vb.dtype), vb).astype(jnp.float32) / l
    lse = (m + jnp.log(l))[..., 0]

    o = o.reshape(Bn, dilation, H, U, hd).transpose(0, 3, 1, 2, 4).reshape(Bn, Sp, H, hd)[:, :S]
    lse = lse.reshape(Bn, dilation, H, U).transpose(0, 3, 1, 2).reshape(Bn, Sp, H)[:, :S]
    return o, lse

def attention_branch(attn_cols, rel_bias):
    Bn, S, _ = attn_cols.shape
    qkv = attn_cols.reshape(Bn, S, N_GROUPS, 3, ATTN_HEADS_PER_GROUP, ATTN_HEAD_DIM)
    outs, lses = [], []
    for g in range(N_GROUPS):
        bias_g = rel_bias[:, g * ATTN_HEADS_PER_GROUP:(g + 1) * ATTN_HEADS_PER_GROUP]
        o, lse = dilated_window_attention(qkv[:, :, g, 0], qkv[:, :, g, 1], qkv[:, :, g, 2],
                                          bias_g, ATTN_DILATIONS[g], ATTN_WINDOWS[g])
        outs.append(o)
        lses.append(lse)
    w = jax.nn.softmax(jnp.stack(lses, axis=0), axis=0)[..., None]
    y = jnp.sum(w * jnp.stack(outs, axis=0), axis=0)
    return y.reshape(Bn, S, ATTN_OUT_WIDTH).astype(attn_cols.dtype)

def hgrn2_chunked(q, k, g, v):
    Bn, H, S, dk = q.shape
    dv = v.shape[-1]
    C = HGRN_CHUNK
    NC = S // C
    q, k, g = (t.reshape(Bn, H, NC, C, dk) for t in (q, k, g))
    v = v.reshape(Bn, H, NC, C, dv)
    G = jnp.cumsum(g, axis=3)
    G_last = G[:, :, :, -1:, :]
    q_t = q * jnp.exp(G)
    k_t = k * jnp.exp(-G)
    k_dec = k * jnp.exp(G_last - G)
    tril = jnp.tril(jnp.ones((C, C), dtype=bool))
    A = jnp.where(tril, jnp.einsum('bhnik,bhnjk->bhnij', q_t, k_t), 0.0)
    o_intra = jnp.einsum('bhnij,bhnjv->bhniv', A, v)

    def step(state, xs):
        qc, kc, glc, vc = xs
        o = jnp.einsum('bhik,bhkv->bhiv', qc, state)
        state = jnp.exp(glc)[:, :, 0, :, None] * state + jnp.einsum('bhjk,bhjv->bhkv', kc, vc)
        return state, o

    xs = tuple(jnp.moveaxis(t, 2, 0) for t in (q_t, k_dec, G_last, v))
    state0 = jnp.zeros((Bn, H, dk, dv), jnp.float32)
    _, o_inter = lax.scan(step, state0, xs)
    o = o_intra + jnp.moveaxis(o_inter, 0, 2)
    return o.reshape(Bn, H, S, dv)

def hgrn2_branch(hg_cols, lb, norm_w):
    Bn, S, _ = hg_cols.shape
    q, f, i, og = jnp.split(hg_cols, 4, axis=-1)

    def heads(t):
        return t.reshape(Bn, S, HGRN_HEADS, -1).transpose(0, 2, 1, 3).astype(jnp.float32)

    lb_h = lb.astype(jnp.float32).reshape(HGRN_HEADS, 1, HGRN_DK)
    q = jax.nn.silu(heads(q))
    f = lb_h + (1.0 - lb_h) * jax.nn.sigmoid(heads(f))
    o = hgrn2_chunked(q, 1.0 - f, jnp.log(f), heads(i))
    o = o * lax.rsqrt(jnp.mean(o * o, axis=-1, keepdims=True) + NORM_EPS) * norm_w.astype(jnp.float32)
    o = o.transpose(0, 2, 1, 3).reshape(Bn, S, HGRN_WIDTH)
    return (o * jax.nn.silu(og.astype(jnp.float32))).astype(hg_cols.dtype)

def conv_ffn(h, w_up, conv_w, conv_b, w_down):
    S = h.shape[1]
    u = h @ w_up
    up = jnp.pad(u, ((0, 0), (CONV_WIDTH - 1, 0), (0, 0)))
    c = conv_b
    for j in range(CONV_WIDTH):
        c = c + conv_w[j] * up[:, j:j + S]
    gate, val = jnp.split(c, 2, axis=-1)
    return (jax.nn.gelu(gate, approximate=False) * val) @ w_down

def setup_inputs(seed: int = 0) -> dict:
    key = jax.random.key(seed)
    ks = jax.random.split(key, 20)
    f32 = jnp.float32

    def nrm(k, shape, scale):
        return jax.random.normal(k, shape, f32) * scale

    def gain(k, shape):
        return 1.0 + 0.05 * jax.random.normal(k, shape, f32)

    return {
        "x": nrm(ks[0], (BATCH, SEQ, D_MODEL), 1.0),
        "pre_mix_norm": gain(ks[1], (DEPTH, D_MODEL)),
        "w_in": nrm(ks[2], (DEPTH, D_MODEL, IN_WIDTH), D_MODEL ** -0.5),
        "rel_bias": nrm(ks[3], (NUM_BUCKETS, N_ATTN_HEADS), 0.5),
        "hgrn_lb_raw": nrm(ks[4], (DEPTH + 1, HGRN_WIDTH), 0.1),
        "hgrn_norm": gain(ks[5], (DEPTH, HGRN_DV)),
        "w_branch_attn": nrm(ks[6], (DEPTH, ATTN_OUT_WIDTH, D_MODEL), ATTN_OUT_WIDTH ** -0.5),
        "w_branch_hgrn": nrm(ks[7], (DEPTH, HGRN_WIDTH, D_MODEL), HGRN_WIDTH ** -0.5),
        "w_out": nrm(ks[8], (DEPTH, D_MODEL, D_MODEL), D_MODEL ** -0.5),
        "post_mix_norm": gain(ks[9], (DEPTH, D_MODEL)),
        "pre_ffn_norm": gain(ks[10], (DEPTH, D_MODEL)),
        "w_up": nrm(ks[11], (DEPTH, D_MODEL, 2 * D_FF), D_MODEL ** -0.5),
        "conv_w": nrm(ks[12], (DEPTH, CONV_WIDTH, 2 * D_FF), CONV_WIDTH ** -0.5),
        "conv_b": nrm(ks[13], (DEPTH, 2 * D_FF), 0.02),
        "w_down": nrm(ks[14], (DEPTH, D_FF, D_MODEL), D_FF ** -0.5),
        "post_ffn_norm": gain(ks[15], (DEPTH, D_MODEL)),
    }

def reference(x, pre_mix_norm, w_in, rel_bias, hgrn_lb_raw, hgrn_norm, w_branch_attn,
              w_branch_hgrn, w_out, post_mix_norm, pre_ffn_norm, w_up, conv_w, conv_b,
              w_down, post_ffn_norm):
    Bn, S, _ = x.shape
    lbs = jnp.cumsum(jax.nn.softmax(hgrn_lb_raw.astype(jnp.float32), axis=0), axis=0)
    split_at = [ATTN_QKV_WIDTH, ATTN_QKV_WIDTH + 4 * HGRN_WIDTH]
    for l in range(DEPTH):
        h = rms_norm(x, pre_mix_norm[l])
        proj = h @ w_in[l]
        attn_cols, hg_cols, gate_cols = jnp.split(proj, split_at, axis=-1)
        y_attn = attention_branch(attn_cols, rel_bias)
        y_hgrn = hgrn2_branch(hg_cols, lbs[l], hgrn_norm[l])
        gates = jax.nn.sigmoid(gate_cols.astype(jnp.float32)).reshape(Bn, S, 2, D_MODEL)
        merged = (gates[:, :, 0] * (y_attn @ w_branch_attn[l])
                  + gates[:, :, 1] * (y_hgrn @ w_branch_hgrn[l])).astype(x.dtype)
        x = x + rms_norm(merged @ w_out[l], post_mix_norm[l])
        h = rms_norm(x, pre_ffn_norm[l])
        x = x + rms_norm(conv_ffn(h, w_up[l], conv_w[l], conv_b[l], w_down[l]), post_ffn_norm[l])
    return x


_drawn_inputs = setup_inputs


def setup_inputs(seed=0):
    import zlib

    import numpy as np

    out = dict(_drawn_inputs(seed))
    spreads = {}
    factors = {'hgrn_lb_raw': 5.24, 'conv_b': 3.453}
    for name, (base, spread) in spreads.items():
        noise = np.random.default_rng([zlib.crc32(name.encode()), seed]).standard_normal(out[name].shape)
        drawn = base * np.exp(spread * noise) if base else spread * noise
        out[name] = __import__('jax').numpy.asarray(drawn.astype(out[name].dtype))
    for name, factor in factors.items():
        out[name] = (out[name] * factor).astype(out[name].dtype)
    return out
```

```python
import math
from contextlib import ExitStack

import numpy as np

import concourse.bass as bass
from concourse import mybir

F32 = mybir.dt.float32
F32R = mybir.dt.float32r
U8 = mybir.dt.uint8
ALU = mybir.AluOpType
ACT = mybir.ActivationFunctionType
AX_X = mybir.AxisListType.X

P = 128
SEQ, DM = 512, 1024
NT = SEQ // P
KC = DM // P
COLS = 512
HEADS, HD = 8, 64
HH = 4
CH = 32
DFF = 2816
FT = DFF // P
UPS = DFF // 256
EPS = 1e-6
NEG = -1e30
GROUPS = (1, 2, 0)
DILATION = (1, 4, 16)
STRIDE = (1, 4, 4)
LINE = 3 * P

SL_HF, SL_HQ, SL_HI, SL_OG = 0, 1, 2, 3
SL_ATT = 4
SL_GATE = SL_ATT + 9
SL_BR = SL_GATE + 4
SL_WO = SL_BR + 2
SL_UP = SL_WO + 2
WO_ORDER = ((0, 0), (1, 0), (0, 1), (1, 1), (2, 0), (2, 1), (3, 0), (3, 1))
WO_COMPLETE = (3, 4, 6, 8)
N_SLOTS = 4 * SL_BR
PAIRS_UP = 4 * SL_UP
PAIRS_DOWN = PAIRS_UP + 4 * UPS
N_PAIRS = PAIRS_DOWN + FT
RAW = 4
RING = 8
DOWN_RING = (0, 1, 2, 3, 10, 11, 4, 5, 6, 7, 8, 9)


def head_slot(a, h):
    return 4 * (SL_ATT + 3 * a + 3) + h


def group_slot(t):
    return 4 * SL_OG + 3 * t


YA_SLOTS = range(N_SLOTS - NT, N_SLOTS)


def attn_at(s):
    for a in range(3):
        if 0 <= s - head_slot(a, 0) < HEADS:
            return a, s - head_slot(a, 0)
    return None


def evacuator(s):
    slab = s // 4
    if slab == SL_HF or slab >= SL_GATE:
        return "act"
    if slab < SL_ATT:
        return "dve"
    return "dve" if (slab - SL_ATT) % 3 == 0 else "act"


def evacuated(s):
    return sum(evacuator(i) == evacuator(s) for i in range(s + 1))


def build(nc, A):
    ctx = ExitStack()
    with ctx:
        base = 16512
        top = [base]

        def place(name, shape, dt, at=None):
            size = int(np.prod(shape[1:])) * (1 if dt == U8 else 4)
            if at is None:
                at = top[0]
                top[0] = at + (size + 31) // 32 * 32
                assert top[0] <= 229368, (name, top[0])
            return nc.alloc_sbuf_tensor_at(name, shape, dt, offset=at)

        def sem(name):
            return ctx.enter_context(nc.semaphore(name))

        KB = 1024
        raw = place("raw", [P, RAW, 2, COLS], F32)
        ws_at = top[0]
        ws = place("ws", [P, 12, 2, 2, COLS], F32R)
        hT = place("hT", [P, 2, KC, SEQ], F32R, ws_at + RING * 8 * KB)
        mT = place("mT", [P, 2, KC, SEQ], F32R, ws_at + RING * 8 * KB)
        ar = top[0]
        top[0] = ar + 92 * KB
        HF = place("HF", [P, HH, SEQ], F32, ar)
        HK = place("HK", [P, HH, SEQ], F32, ar + 8 * KB)
        HQ = place("HQ", [P, HH, SEQ], F32, ar + 16 * KB)
        HKX = place("HKX", [P, HH, SEQ], F32, ar + 24 * KB)
        HV = place("HV", [P, NT, COLS], F32, ar + 32 * KB)
        HOG = place("HOG", [P, NT, COLS], F32, ar + 40 * KB)
        scan_mask = place("scan_mask", [P, SEQ], F32, ar + 56 * KB)
        E1 = place("E1", [P, SEQ], F32, ar + 58 * KB)
        E2 = place("E2", [P, SEQ], F32, ar + 60 * KB)
        E3 = place("E3", [P, SEQ], F32, ar + 62 * KB)
        mask_f = place("mask_f", [P, P], F32, ar + 66 * KB)
        carry = place("carry", [P, 2, HH, P], F32, ar + 56 * KB)
        states = place("states", [P, HH, 3, P], F32, ar + 60 * KB)
        AT = place("AT", [P, HH, P], F32, ar + 84 * KB)
        kd = place("kd", [P, HH, P], F32, ar + 86 * KB)
        yo = place("yo", [P, HH, P], F32, ar + 88 * KB)
        junk_h = place("junk_h", [P, P], F32, ar + 90 * KB)
        yh_hi = place("yh_hi", [P, HH, SEQ], F32R, ar + 68 * KB)
        yh_lo = place("yh_lo", [P, HH, SEQ], F32R, ar + 76 * KB)
        QT = place("QT", [P, 4, SEQ], F32, ar)
        KT = place("KT", [P, 4, SEQ], F32, ar + 8 * KB)
        bias_a = place("bias_a", [P, HEADS, P], F32, ar + 16 * KB)
        bias_b = place("bias_b", [P, HEADS, P], F32, ar + 20 * KB)
        bias_c = place("bias_c", [P, HEADS, 2 * P], F32, ar + 16 * KB)
        O = place("O", [P, NT, COLS], F32, ar + 24 * KB)
        PR = place("PR", [P, 2, NT, 2 * P], F32, ar + 32 * KB)
        VB = place("VB", [P, NT, COLS], F32, ar + 40 * KB)
        VA = place("VA", [P, NT, COLS], F32, ar + 48 * KB)
        PT = place("PT", [P, 8, P], F32, ar + 56 * KB)
        On0 = place("On0", [P, NT, COLS], F32, ar + 40 * KB)
        On1 = place("On1", [P, NT, COLS], F32, ar + 32 * KB)
        ya_hi = place("ya_hi", [P, 4, SEQ], F32R, ar + 16 * KB)
        ya_lo = place("ya_lo", [P, 4, SEQ], F32R, ar + 48 * KB)
        gates = [place("gate0a", [P, 4, SEQ], F32, ar + 60 * KB), place("gate1a", [P, 4, SEQ], F32, ar + 84 * KB),
                 place("gate0b", [P, 4, SEQ], F32, ar), place("gate1b", [P, 4, SEQ], F32, ar + 8 * KB)]
        m1 = place("m1", [P, SEQ], F32, ar + 56 * KB)
        m2 = place("m2", [P, SEQ], F32, ar + 58 * KB)
        x_in = place("x_in", [P, NT, DM], F32, ar)
        w_pre = place("w_pre", [P, DM], F32, ar + 16 * KB)
        xn = place("xn", [P, 2, DM], F32, ar + 20 * KB)
        onehot = place("onehot", [32, 3, LINE], F32, ar + 28 * KB)
        line_add = place("line_add", [HEADS, 3, LINE], F32, ar + 33 * KB)
        lines = place("lines", [HEADS, 3, LINE], F32, ar + 38 * KB)
        rel = place("rel", [32, 3 * HEADS], F32, ar + 43 * KB)
        junk_x = place("junk_x", [P, DM], F32, ar + 44 * KB)
        x2 = place("x2", [P, NT, DM], F32, ar + 76 * KB)
        h2_hi = place("h2_hi", [P, KC, SEQ], F32R, ar)
        h2_lo = place("h2_lo", [P, KC, SEQ], F32R, ar + 16 * KB)
        w_post = place("w_post", [P, DM], F32, ar + 32 * KB)
        w_pre2 = place("w_pre2", [P, DM], F32, ar + 36 * KB)
        mixed = place("mixed", [P, DM], F32, ar + 40 * KB)
        xn2 = place("xn2", [P, DM], F32, ar + 44 * KB)
        junk_w = place("junk_w", [P, DM], F32, ar + 48 * KB)
        aT = place("aT", [P, FT, SEQ], F32, ar + 32 * KB)
        conv_at = ws_at + RING * 8 * KB
        up = [place("up_gate", [P, SEQ + 2], F32, conv_at), place("up_val", [P, SEQ + 2], F32, conv_at + 2080)]
        cv = [place("cv_gate", [P, SEQ], F32, conv_at + 5 * KB), place("cv_val", [P, SEQ], F32, conv_at + 7 * KB)]
        ge = place("ge", [P, SEQ], F32, conv_at + 9 * KB)
        a_hi = place("a_hi", [P, 4, SEQ], F32R, ar)
        a_lo = place("a_lo", [P, 4, SEQ], F32R, ar + 8 * KB)
        d0 = place("d0", [P, NT, COLS], F32, ar + 16 * KB)
        w_ffn = place("w_ffn", [P, DM], F32, ar + 24 * KB)
        res = [place("res0", [P, DM], F32, ar + 28 * KB), place("res1", [P, DM], F32, ar + 32 * KB)]
        junk_d = place("junk_d", [P, COLS], F32, ar + 36 * KB)
        ident = place("ident", [P, P], F32)
        h_norm = place("h_norm", [P, P], F32)
        chunk_mask = place("chunk_mask", [P, P], U8)
        cw = place("cw", [P, 4, 2 * FT], F32)
        stat = place("stat", [P, 3, NT, 2 * HEADS], F32)
        tmp = place("tmp", [P, 4, NT, HEADS], F32)
        chunk_decay = place("chunk_decay", [P, HH, SEQ // CH], F32)
        lb = place("lb", [P, 2, HH], F32)
        lb_a = place("lb_a", [P, HH], F32)
        lb_b = place("lb_b", [P, HH], F32)
        ss = place("ss", [P, 8], F32)
        var = place("var", [P, 4], F32)
        rstd = place("rstd", [P, 4], F32)
        minus_half = place("minus_half", [P, 4], F32)
        mx = place("mx", [P, 4], F32)

        ps = ctx.enter_context(nc.psum_tensor("ps", [P, 8, COLS], F32))

        def bank(b, n=1):
            return ps[:, b, :] if n == 1 else ps[:, b:b + n, :]

        def quarters(b):
            return ps[:, b, :].rearrange("p (q c) -> p q c", q=4)

        pt_banks = ps[:, 4:6, :].rearrange("p b (n k) -> p (b n) k", n=4)
        scores2 = ps[:, 2:4, :].rearrange("p b (n k) -> p (b n) k", n=2)

        def low_hT(t, tell):
            cols = slice(t * P, (t + 1) * P)
            tell(nc.vector.tensor_tensor(hT[:, 1, :, cols], bank(2 + 2 * (t % 2), 2).rearrange("p b (k c) -> p (b k) c", c=P),
                                         hT[:, 0, :, cols].bitcast(F32), ALU.subtract), hT_ready)

        raw_landed = [sem(f"raw_landed{i}") for i in range(RAW)]
        hi_done, lo_done = sem("hi_done"), sem("lo_done")
        x_landed = [sem(f"x_landed{i}") for i in range(NT)]
        const_landed, lb_landed, rel_landed = sem("const_landed"), sem("lb_landed"), sem("rel_landed")
        act_step, dve_step, pool_step = sem("act_step"), sem("dve_step"), sem("pool_step")
        line_done, line_ready, line_stored = sem("line_done"), sem("line_ready"), sem("line_stored")
        ssq_ready, var_ready, rstd_ready = sem("ssq_ready"), sem("var_ready"), sem("rstd_ready")
        xn_ready, xt_done, hT_hi, hT_ready = sem("xn_ready"), sem("xt_done"), sem("hT_hi"), sem("hT_ready")
        proj_done, evac = sem("proj_done"), {"act": sem("proj_free_act"), "dve": sem("proj_free_dve")}
        tanh_ready, f_ready, log_ready = sem("tanh_ready"), sem("f_ready"), sem("log_ready")
        G_ready, dif_ready, exps_ready, prep_done = sem("G_ready"), sem("dif_ready"), sem("exps_ready"), sem("prep_done")
        at_done, at_ready, kdt_done, kd_ready = sem("at_done"), sem("at_ready"), sem("kdt_done"), sem("kd_ready")
        kv_done, chain_done, o_done, o_read = sem("kv_done"), sem("chain_done"), sem("o_done"), sem("o_read")
        yo_ready, yht_done, yh_hi_done, yh_split = sem("yo_ready"), sem("yht_done"), sem("yh_hi_done"), sem("yh_split")
        bias_landed = [sem(f"bias_landed{a}") for a in range(3)]
        scores_done, max_ready, exp_done = sem("scores_done"), sem("max_ready"), sem("exp_done")
        pt_done, pt_ready, pv_done, o_saved = sem("pt_done"), sem("pt_ready"), sem("pv_done"), sem("o_saved")
        O_stored, On_landed = [sem(f"O_stored{a}") for a in range(2)], [sem(f"On_landed{a}") for a in range(2)]
        dif_lse, exp_lse = sem("dif_lse"), sem("exp_lse")
        ya_ready, yat_done, ya_hi_done, ya_split = sem("ya_ready"), sem("yat_done"), sem("ya_hi_done"), sem("ya_split")
        br_done, br_read, m_ready, m_hi, m_split = sem("br_done"), sem("br_read"), sem("m_ready"), sem("m_hi"), sem("m_split")
        x2_landed, wn_landed = sem("x2_landed"), sem("wn_landed")
        wo_done, wo_ssq, wo_read, wo_res = sem("wo_done"), sem("wo_ssq"), sem("wo_read"), sem("wo_res")
        xn2_ready, h2t_done, h2_hi_done, h2_split = sem("xn2_ready"), sem("h2t_done"), sem("h2_hi_done"), sem("h2_split")
        up_done, up_copied, tap0_done, conv_done, gelu_done, a_ready = (
            sem("up_done"), sem("up_copied"), sem("tap0_done"), sem("conv_done"), sem("gelu_done"), sem("a_ready"))
        pads_ready, tap1_done = sem("pads_ready"), sem("tap1_done")
        a_hi_done, a_split, down_chunk, down_tile = sem("a_hi_done"), sem("a_split"), sem("down_chunk"), sem("down_tile")
        d0_ready, fin_ssq, out_ready, out_stored, wf_landed = (
            sem("d0_ready"), sem("fin_ssq"), sem("out_ready"), [sem(f"out_stored{i}") for i in range(2)], sem("wf_landed"))

        block = ctx.enter_context(nc.Block())

        def teller(eng, step):
            told = {}

            def tell(ins, s):
                ins.then_inc(s, 1)
                told[id(s)] = told.get(id(s), 0) + 1
                eng.wait_ge(s, told[id(s)])

            return (lambda ins: tell(ins, step)), tell

        @block.sync
        def _(sp):
            def load(n, r):
                sp.dma_start(raw[:, r, :, :], A["stream"][n, :, :, :]).then_inc(raw_landed[r], 16)

            for r in range(RAW):
                load(r, r)
            with sp.Fori(1, N_PAIRS // RAW) as g:
                for r in range(RAW):
                    sp.wait_ge(hi_done, RAW * g + (r + 1 - RAW))
                    sp.wait_ge(lo_done, RAW * g + (r + 1 - RAW))
                    load(RAW * g + r, r)
            for n in range(N_PAIRS // RAW * RAW, N_PAIRS):
                sp.wait_ge(hi_done, n - RAW + 1)
                sp.wait_ge(lo_done, n - RAW + 1)
                load(n, n % RAW)
            for t in range(NT):
                sp.wait_ge(out_ready, t + 1)
                sp.dma_start(A["out"][t * P:(t + 1) * P, :], res[t % 2][:, :]).then_inc(out_stored[t % 2], 16)
            for r in range(2):
                sp.wait_ge(out_stored[r], 16 * NT // 2)

        def split_place(n):
            return n % RING if n < PAIRS_DOWN else DOWN_RING[(n - PAIRS_DOWN) % 12]

        @block.gpsimd
        def _(pool):
            roots = [0]

            def low(n):
                pool.wait_ge(hi_done, n + 1)
                w = split_place(n)
                pool.tensor_tensor(ws[:, w, 1, :, :], raw[:, n % RAW, :, :], ws[:, w, 0, :, :].bitcast(F32),
                                   ALU.subtract).then_inc(lo_done, 1)

            def root(n):
                roots[0] += 1
                pool.wait_ge(var_ready, roots[0])
                pool.tensor_tensor(rstd[:, 0:n], var[:, 0:n], minus_half[:, 0:n], ALU.pow).then_inc(rstd_ready, 1)

            pool.memset(minus_half[:, :], -0.5).then_inc(pool_step, 1)
            pool.wait_ge(pool_step, 1)
            for t in range(NT):
                root(1)
                low(t)
            for s in range(N_SLOTS):
                low(4 + s)
                for t in range(NT):
                    if s == group_slot(t) + 2:
                        root(HH)
            for n in range(N_SLOTS + 4, PAIRS_UP):
                low(n)
            for t in range(NT):
                if t == NT - 1:
                    for r in range(4):
                        low(PAIRS_UP + r)
                root(1)
                root(1)
            first = PAIRS_UP + 4
            with pool.Fori(0, (UPS - 1) // 2) as g:
                for r in range(RING):
                    q = first + r
                    pool.wait_ge(hi_done, RING * g + (q + 1))
                    w = split_place(q)
                    pool.tensor_tensor(ws[:, w, 1, :, :], raw[:, q % RAW, :, :],
                                       ws[:, w, 0, :, :].bitcast(F32), ALU.subtract).then_inc(lo_done, 1)
            for n in range(PAIRS_DOWN, N_PAIRS):
                low(n)
            for t in range(NT):
                root(1)

        @block.scalar
        def _(act):
            run, tell = teller(act, act_step)
            stepped = [0]

            def hi(n):
                act.wait_ge(raw_landed[n % RAW], 16 * (n // RAW + 1))
                m = n - PAIRS_DOWN
                before = n // 4 - 2
                if before < 0:
                    pass
                elif before < SL_BR:
                    act.wait_ge(proj_done, 4 * (before + 1))
                elif before < SL_WO:
                    act.wait_ge(br_done, KC * (before - SL_BR + 1))
                elif before == SL_WO:
                    act.wait_ge(wo_done, 2 * NT - 1)
                elif before == SL_WO + 1:
                    act.wait_ge(wo_done, 2 * NT)
                elif m < 4:
                    act.wait_ge(up_done, 4 * (before - SL_UP + 1))
                elif 6 <= m < 10:
                    act.wait_ge(up_done, 4 * UPS)
                elif 10 <= m < 12:
                    act.wait_ge(a_ready, FT)
                elif m >= 12:
                    act.wait_ge(down_chunk, 2 * (m - 11))
                tell(act.activation(ws[:, split_place(n), 0, :, :], raw[:, n % RAW, :, :], ACT.Copy), hi_done)

            for t in range(NT):
                act.dma_start(x_in[:, t, :], A["x"][t * P:(t + 1) * P, :]).then_inc(x_landed[t], 16)
                if t == 0:
                    act.dma_start(rel[:, :], A["rel_bias"]).then_inc(rel_landed, 16)
                    act.dma_start(onehot[:, :, :], A["onehot"]).then_inc(rel_landed, 16)
                    act.dma_start(line_add[:, :, :], A["line_add"]).then_inc(rel_landed, 16)
                    act.dma_start(w_pre[:, :], A["pre_mix"].partition_broadcast(P)).then_inc(const_landed, 16)
                    act.dma_start(ident[:, :], A["ident"]).then_inc(const_landed, 16)
            act.dma_start(lb[:, :, :], A["lb_raw"]).then_inc(lb_landed, 16)
            act.dma_start(scan_mask[:, :], A["scan_mask"]).then_inc(lb_landed, 16)
            act.dma_start(h_norm[:, :], A["hgrn_norm"].partition_broadcast(P)).then_inc(lb_landed, 16)
            act.dma_start(mask_f[:, :], A["chunk_mask"]).then_inc(lb_landed, 16)
            act.dma_start(cw[:, :, :], A["conv"]).then_inc(lb_landed, 16)
            for t in range(NT):
                act.wait_ge(x_landed[t], 16)
                tell(act.activation(junk_x[:, :], x_in[:, t, :], ACT.Square, accum_out=ss[:, t:t + 1]), ssq_ready)
                hi(t)
            act.wait_ge(dve_step, 1)
            run(act.activation(lb_b[:, :], lb_a[:, :], ACT.Tanh, scale=0.5))
            act.wait_ge(line_ready, 3)
            for a, g in enumerate(GROUPS):
                keys = A["table_scratch"][a].shape[2]
                line = lines[:, g, 2 * P - keys:]
                act.dma_start(A["table_scratch"][a].rearrange("p h j -> h p j"),
                              bass.AP(line.tensor, line.offset + P - 1, [line.ap[0], [-1, P], [1, keys]])
                              ).then_inc(line_stored, 16)
            for t in range(NT):
                act.wait_ge(xt_done, t + 1)
                b = 2 + 2 * (t % 2)
                tell(act.activation(hT[:, 0, :, t * P:(t + 1) * P],
                                    bank(b, 2).rearrange("p b (k c) -> p (b k) c", c=P), ACT.Copy), hT_hi)

            def slot_act(s):
                slab, i = divmod(s, 4)
                hi(4 * (slab + 1) + i)
                if s == 4 * SL_HQ:
                    act.wait_ge(f_ready, HH)
                    tell(act.activation(HF[:, :, :], HF[:, :, :], ACT.Ln), log_ready)
                if slab == SL_HI:
                    h = i
                    if h:
                        act.wait_ge(prep_done, h)
                    act.wait_ge(G_ready, h + 1)
                    run(act.activation(E1[:, :], HF[:, h, :], ACT.Exp))
                    run(act.activation(E2[:, :], HF[:, h, :], ACT.Exp, scale=-1.0))
                    run(act.activation(chunk_decay[:, h, :],
                                       HF[:, h, :].rearrange("p (c j) -> p c j", j=CH)[:, :, CH - 1], ACT.Exp))
                    act.wait_ge(dif_ready, h + 1)
                    tell(act.activation(E3[:, :], E3[:, :], ACT.Exp), exps_ready)
                for t in range(NT):
                    if s == group_slot(t):
                        act.wait_ge(kdt_done, t + 1)
                        if t:
                            act.wait_ge(kv_done, t)
                        tell(act.activation(kd[:, :, :], quarters(3), ACT.Copy), kd_ready)
                for t in range(NT):
                    if s == group_slot(t) + 3:
                        act.wait_ge(yht_done, t + 1)
                        tell(act.activation(yh_hi[:, :, t * P:(t + 1) * P], quarters(3), ACT.Copy), yh_hi_done)
                    if s == group_slot(t) + 2:
                        act.wait_ge(o_done, HH * (t + 1))
                        if t:
                            act.wait_ge(rstd_ready, NT + t)
                        for h in range(HH):
                            ins = act.activation(junk_h[:, :], quarters(2)[:, h, :], ACT.Square, accum_out=ss[:, h:h + 1])
                            tell(ins, ssq_ready) if h == HH - 1 else run(ins)
                ah = attn_at(s)
                if ah:
                    a, h = ah
                    idx = HEADS * a + h
                    act.wait_ge(max_ready, idx + 1)
                    if idx >= 2:
                        act.wait_ge(pt_done, idx - 1)
                    for n in range(NT):
                        src = scores2[:, n, :] if a == 2 else quarters(2)[:, n, :]
                        dst = PR[:, idx % 2, n, P:]
                        if a == 2 and n == 0:
                            src = scores2[:, n, P:]
                        elif a == 2:
                            dst = PR[:, idx % 2, n, :]
                        ins = act.activation(dst, src, ACT.Exp, bias=stat[:, a, n, h:h + 1],
                                             accum_out=stat[:, a, n, HEADS + h:HEADS + h + 1])
                        tell(ins, exp_done) if n == NT - 1 else run(ins)
                for a in range(2):
                    if s == head_slot(a, HEADS - 1) + 3:
                        act.wait_ge(o_saved, HEADS * (a + 1))
                        for src, dst in ((O[:, :, :], A["O_scratch"][a, :, :]), (stat[:, a, :, :], A["stat_scratch"][a, :, :])):
                            act.dma_start(dst.rearrange("(p n) c -> p n c", n=NT), src).then_inc(O_stored[a], 16)
                    if s == (head_slot(1, HEADS - 1) + 4, head_slot(2, HEADS - 1) + 2)[a]:
                        act.wait_ge(O_stored[a], 32)
                        act.wait_ge(pv_done, 16) if a == 0 else act.wait_ge(pt_done, 24)
                        act.dma_start((On0, On1)[a][:, :, :], A["O_scratch"][a, :, :].rearrange("(t p) c -> p t c", p=P)
                                      ).then_inc(On_landed[a], 16)
                        act.dma_start(stat[:, a, :, :], A["stat_scratch"][a, :, :].rearrange("(t p) c -> p t c", p=P)
                                      ).then_inc(On_landed[a], 16)
                if s == head_slot(0, 0) - 2:
                    act.wait_ge(o_done, HH * NT)
                    act.wait_ge(line_stored, 48)
                    dma_bias(0)
                if s == head_slot(0, 0) - 1:
                    dma_bias(1)
                if s == head_slot(1, HEADS - 1) + 3:
                    act.wait_ge(max_ready, 2 * HEADS)
                    dma_bias(2)
                if s == head_slot(2, HEADS - 1) + 3:
                    act.wait_ge(dif_lse, 1)
                    tell(act.activation(tmp[:, 0:3, :, :], tmp[:, 0:3, :, :], ACT.Exp), exp_lse)
                if s in YA_SLOTS:
                    t = s - YA_SLOTS[0]
                    act.wait_ge(yat_done, t + 1)
                    tell(act.activation(ya_hi[:, :, t * P:(t + 1) * P], quarters(7), ACT.Copy), ya_hi_done)
                act_block(s)

            def dma_bias(a):
                act.dma_start((bias_a, bias_b, bias_c)[a][:, :, :], A["table_scratch"][a]).then_inc(bias_landed[a], 16)

            def act_block(s):
                slab, i = divmod(s, 4)
                src = bank(s % 2)
                act.wait_ge(proj_done, s + 1)
                if slab == SL_HF:
                    tell(act.activation(HF[:, i, :], src, ACT.Tanh, scale=0.5), evac["act"])
                elif slab == SL_HQ:
                    tell(act.activation(HQ[:, i, :], src, ACT.Tanh, scale=0.5), tanh_ready)
                elif slab == SL_OG:
                    tell(act.activation(HOG[:, i, :], src, ACT.Tanh, scale=0.5), tanh_ready)
                elif slab >= SL_GATE:
                    if slab == SL_GATE + 1 and i == 0:
                        act.wait_ge(yh_split, NT)
                    if slab == SL_GATE + 2 and i == 0:
                        act.wait_ge(scores_done, 3 * HEADS)
                    tell(act.activation(gates[slab - SL_GATE][:, i, :], src, ACT.Tanh, scale=0.5), evac["act"])
                elif slab >= SL_ATT and (slab - SL_ATT) % 3:
                    a, which = divmod(slab - SL_ATT, 3)
                    if a:
                        act.wait_ge(scores_done, HEADS * (a - 1) + (2 * i + 2 if which == 1 else HEADS))
                    elif which == 1:
                        act.wait_ge(prep_done, HH)
                    else:
                        act.wait_ge(o_done, HH * NT)
                    d = STRIDE[GROUPS[a]]
                    dst = (QT if which == 1 else KT)[:, i, :]
                    if d > 1:
                        dst = dst.rearrange("p (r u) -> p r u", r=d)
                        src = src.rearrange("p (u r) -> p r u", r=d)
                    tell(act.activation(dst, src, ACT.Copy), evac["act"])

            for s in range(N_SLOTS):
                slot_act(s)

            for j in range(KC):
                hi(N_SLOTS + 4 + j)
                act.wait_ge(m_ready, j + 1)
                tell(act.activation(mT[:, 0, j, :], m1[:, :], ACT.Copy, scale=0.5), m_hi)
            act.wait_ge(br_done, 2 * KC)
            act.dma_start(x2[:, :, :], A["x"].rearrange("(t p) c -> p t c", p=P)).then_inc(x2_landed, 16)
            act.dma_start(w_post[:, :], A["post_mix"].partition_broadcast(P)).then_inc(wn_landed, 16)
            act.dma_start(w_pre2[:, :], A["pre_ffn"].partition_broadcast(P)).then_inc(wn_landed, 16)
            for r in range(4):
                hi(PAIRS_UP - 4 + r)

            def split_h2(t):
                act.wait_ge(h2t_done, t + 1)
                tell(act.activation(h2_hi[:, :, t * P:(t + 1) * P],
                                    bank(4 + 2 * (t % 2), 2).rearrange("p b (k c) -> p (b k) c", c=P), ACT.Copy), h2_hi_done)

            for t in range(NT):
                if t == NT - 1:
                    for r in range(4):
                        hi(PAIRS_UP + r)
                act.wait_ge(wo_done, WO_COMPLETE[t])
                if t == 0:
                    act.wait_ge(m_split, KC)
                tell(act.activation(junk_w[:, :], ps[:, 2 * (t % 2):2 * (t % 2) + 2, :].rearrange("p b c -> p (b c)"),
                                    ACT.Square, accum_out=ss[:, t:t + 1]), wo_ssq)
                act.wait_ge(wo_res, t + 1)
                tell(act.activation(junk_w[:, :], x2[:, t, :], ACT.Square, accum_out=ss[:, NT + t:NT + t + 1]), wo_ssq)
                if t:
                    split_h2(t - 1)
            split_h2(NT - 1)

            def up_tile(f, k, after_first):
                for half in range(2):
                    act.wait_ge(up_done, 2 * f + (half + 1))
                    if after_first:
                        act.wait_ge(conv_done, 2 * f + (half - 1))
                    act.activation(up[half][:, 2:], bank(2 * k + half), ACT.Copy).then_inc(up_copied, 1)
                    act.wait_ge(up_copied, 2 * f + (half + 1))
                    if after_first:
                        act.wait_ge(a_ready, f)
                    c = f + half * FT
                    act.activation(cv[half][:, :], up[half][:, 0:SEQ], ACT.Identity,
                                   scale=cw[:, 0, bass.ds(c, 1)], bias=cw[:, 3, bass.ds(c, 1)]).then_inc(tap0_done, 1)
                act.wait_ge(conv_done, 2 * f + 1)
                act.activation(ge[:, :], cv[0][:, :], ACT.Gelu).then_inc(gelu_done, 1)

            act.wait_ge(pads_ready, 2)
            for k in range(2):
                for r in range(2):
                    hi(PAIRS_UP + 4 + 2 * k + r)
                up_tile(k, k, k > 0)
            first = PAIRS_UP + RING
            with act.Fori(0, (UPS - 1) // 2) as g:
                for k in range(4):
                    for r in range(2):
                        q = first + 2 * k + r
                        act.wait_ge(raw_landed[q % RAW], 32 * g + 16 * (q // RAW + 1))
                        act.wait_ge(up_done, 8 * g + 4 * (k // 2 + 1))
                        act.activation(ws[:, q % RING, 0, :, :], raw[:, q % RAW, :, :], ACT.Copy).then_inc(hi_done, 1)
                    up_tile(4 * g + (2 + k), k % 2, True)

            act.wait_ge(up_done, 4 * UPS)
            act.dma_start(w_ffn[:, :], A["post_ffn"].partition_broadcast(P)).then_inc(wf_landed, 16)
            for q in range(2 * FT):
                if q % 2 == 0 and PAIRS_DOWN + 4 + q // 2 < N_PAIRS:
                    n = PAIRS_DOWN + 4 + q // 2
                    m = n - PAIRS_DOWN
                    act.wait_ge(raw_landed[n % RAW], 16 * (n // RAW + 1))
                    if 10 <= m < 12:
                        act.wait_ge(a_ready, FT)
                    elif m >= 12:
                        act.wait_ge(down_chunk, 2 * (m - 11))
                    act.activation(ws[:, split_place(n), 0, :, :], raw[:, n % RAW, :, :], ACT.Copy).then_inc(hi_done, 1)
                act.wait_ge(a_ready, min(q + 1, FT))
                if q >= 4:
                    act.wait_ge(down_chunk, q - 3)
                act.activation(a_hi[:, q % 4, :], aT[:, q % FT, :], ACT.Copy).then_inc(a_hi_done, 1)
                t = q - FT - 2
                if 0 <= t < NT:
                    act.wait_ge(d0_ready, t + 1)
                    act.activation(res[0][:, 0:COLS], d0[:, t, :], ACT.Square, accum_out=ss[:, t:t + 1]).then_inc(fin_ssq, 1)
                    act.wait_ge(fin_ssq, t + 1)
            act.wait_ge(a_split, 2 * FT)
            for t in range(NT):
                act.wait_ge(down_tile, t + 1)
                act.activation(junk_d[:, :], bank(4 + t), ACT.Square, accum_out=ss[:, NT + t:NT + t + 1]).then_inc(fin_ssq, 1)
                act.wait_ge(fin_ssq, NT + t + 1)

        @block.vector
        def _(dve):
            run, tell = teller(dve, dve_step)
            roots = [0]

            def root(ssq, width, n, extra=None):
                if extra is not None:
                    run(dve.tensor_tensor(var[:, 0:n], ssq, extra, ALU.add))
                    ssq = var[:, 0:n]
                tell(dve.tensor_scalar(var[:, 0:n], ssq, 1.0 / width, EPS, ALU.mult, ALU.add), var_ready)
                roots[0] += 1
                dve.wait_ge(rstd_ready, roots[0])

            dve.wait_ge(lb_landed, 80)
            run(dve.tensor_tensor(lb_a[:, :], lb[:, 0, :], lb[:, 1, :], ALU.subtract))
            run(dve.tensor_copy(chunk_mask[:, :], mask_f[:, :]))
            for t in range(NT):
                dve.wait_ge(ssq_ready, t + 1)
                root(ss[:, t:t + 1], DM, 1)
                if t == 0:
                    dve.wait_ge(const_landed, 32)
                if t >= 2:
                    dve.wait_ge(xt_done, t - 1)
                tell(dve.scalar_tensor_tensor(xn[:, t % 2, :], x_in[:, t, :], rstd[:, 0:1], w_pre[:, :],
                                              ALU.mult, ALU.mult), xn_ready)
                if t == 1:
                    dve.wait_ge(rel_landed, 48)
                    for g in range(3):
                        dve.wait_ge(line_done, g + 1)
                        tell(dve.tensor_tensor(lines[:, g, :], ps[0:HEADS, (6, 7, 0)[g], 0:LINE], line_add[:, g, :],
                                               ALU.add), line_ready)
                if t >= 1:
                    u = t - 1
                    dve.wait_ge(hT_hi, u + 1)
                    low_hT(u, tell)
            dve.wait_ge(hT_hi, NT)
            low_hT(NT - 1, tell)
            dve.wait_ge(act_step, 1)
            run(dve.tensor_scalar(lb_a[:, :], lb_b[:, :], -0.25, 0.25, ALU.mult, ALU.add))
            run(dve.tensor_scalar(lb_b[:, :], lb_b[:, :], 0.25, 0.75, ALU.mult, ALU.add))

            def slot_dve(s):
                slab, i = divmod(s, 4)
                if slab == SL_HI:
                    h = i
                    if h == 0:
                        dve.wait_ge(log_ready, 1)
                    tell(dve.tensor_tensor_scan(HF[:, h, :], scan_mask[:, :], HF[:, h, :], 0.0, ALU.mult, ALU.add), G_ready)
                    G = HF[:, h, :].rearrange("p (c j) -> p c j", j=CH)
                    tell(dve.tensor_tensor(E3[:, :].rearrange("p (c j) -> p c j", j=CH),
                                           G[:, :, CH - 1:CH].to_broadcast([P, SEQ // CH, CH]), G, ALU.subtract), dif_ready)
                    dve.wait_ge(exps_ready, h + 1)
                    run(dve.scalar_tensor_tensor(HQ[:, h, :], HQ[:, h, :], 0.5, E1[:, :], ALU.mult, ALU.mult))
                    run(dve.tensor_tensor(HKX[:, h, :], HK[:, h, :], E2[:, :], ALU.mult))
                    tell(dve.tensor_tensor(HK[:, h, :], HK[:, h, :], E3[:, :], ALU.mult), prep_done)
                for t in range(NT):
                    if s == group_slot(t):
                        if t == 0:
                            run(dve.memset(carry[:, 0, :, :], 0.0))
                            run(dve.memset(AT[:, :, :], 0.0))
                        else:
                            dve.wait_ge(o_done, HH * t)
                        dve.wait_ge(at_done, t + 1)
                        tell(dve.copy_predicated(AT[:, :, :], chunk_mask[:, :].unsqueeze(1).to_broadcast([P, HH, P]),
                                                 quarters(2)), at_ready)
                        dve.wait_ge(kv_done, t + 1)
                        for h in range(HH):
                            for c in range(4):
                                old = carry[:, t % 2, h, :] if c == 0 else states[:, h, c - 1, :]
                                new = carry[:, (t + 1) % 2, h, :] if c == 3 else states[:, h, c, :]
                                ins = dve.scalar_tensor_tensor(new, old, chunk_decay[:, h, 4 * t + c:4 * t + c + 1],
                                                               quarters(4 + c)[:, h, :], ALU.mult, ALU.add)
                                tell(ins, chain_done) if c == 3 else run(ins)
                for t in range(NT):
                    if s == group_slot(t) + 3:
                        dve.wait_ge(yh_hi_done, t + 1)
                        tell(dve.tensor_tensor(yh_lo[:, :, t * P:(t + 1) * P], quarters(3),
                                               yh_hi[:, :, t * P:(t + 1) * P].bitcast(F32), ALU.subtract), yh_split)
                    if s == group_slot(t) + 2:
                        dve.wait_ge(ssq_ready, NT + t + 1)
                        root(ss[:, 0:HH], P, HH)
                        if t:
                            dve.wait_ge(yht_done, t)
                        tell(dve.tensor_tensor(yo[:, :, :], quarters(2), rstd[:, 0:HH].unsqueeze(2).to_broadcast([P, HH, P]),
                                               ALU.mult), o_read)
                        run(dve.tensor_tensor(yo[:, :, :], yo[:, :, :], h_norm[:, :].unsqueeze(1).to_broadcast([P, HH, P]),
                                              ALU.mult))
                        tell(dve.scalar_tensor_tensor(yo[:, :, :].rearrange("p h c -> p (h c)"),
                                                      yo[:, :, :].rearrange("p h c -> p (h c)"), 0.5, HOG[:, t, :],
                                                      ALU.mult, ALU.mult), yo_ready)
                if s >= 2 and attn_at(s - 2):
                    a, h = attn_at(s - 2)
                    dve.wait_ge(pv_done, HEADS * a + h + 1)
                    if a and h == 0:
                        dve.wait_ge(O_stored[a - 1], 32)
                    tell(dve.tensor_copy(O[:, :, h * HD:(h + 1) * HD],
                                         ps[:, 6, 0:NT * HD].rearrange("p (n d) -> p n d", n=NT)), o_saved)
                if attn_at(s):
                    a, h = attn_at(s)
                    if h == 0:
                        dve.wait_ge(bias_landed[a], 16)
                    dve.wait_ge(scores_done, HEADS * a + h + 1)
                    if a == 2:
                        run(dve.scalar_tensor_tensor(scores2[:, 0, P:], scores2[:, 0, P:], HD ** -0.5, bias_c[:, h, P:],
                                                     ALU.mult, ALU.add))
                        run(dve.scalar_tensor_tensor(scores2[:, 1:, :], scores2[:, 1:, :], HD ** -0.5,
                                                     bias_c[:, h, :].unsqueeze(1).to_broadcast([P, NT - 1, 2 * P]),
                                                     ALU.mult, ALU.add))
                        run(dve.tensor_reduce(mx[:, 0:1], scores2[:, 0, P:], AX_X, ALU.max))
                        run(dve.tensor_reduce(mx[:, 1:], scores2[:, 1:, :], AX_X, ALU.max))
                    else:
                        table = (bias_a, bias_b)[a]
                        run(dve.scalar_tensor_tensor(quarters(2), quarters(2), HD ** -0.5,
                                                     table[:, h, :].unsqueeze(1).to_broadcast([P, NT, P]),
                                                     ALU.mult, ALU.add))
                        run(dve.tensor_reduce(mx[:, :], quarters(2), AX_X, ALU.max))
                    tell(dve.tensor_scalar(stat[:, a, :, h], mx[:, :], -1.0, None, ALU.mult), max_ready)
                if s >= 1 and attn_at(s - 1):
                    a, h = attn_at(s - 1)
                    idx = HEADS * a + h
                    dve.wait_ge(pt_done, idx + 1)
                    if idx:
                        dve.wait_ge(pv_done, idx)
                    k = 7 if a == 2 else 4
                    tell(dve.tensor_copy(PT[:, 0:k, :], pt_banks[:, 0:k, :]), pt_ready)
                if s == head_slot(2, HEADS - 1) + 3:
                    dve.wait_ge(On_landed[0], 32)
                    dve.wait_ge(On_landed[1], 32)
                    low, lse = [stat[:, a, :, 0:HEADS] for a in range(3)], [stat[:, a, :, HEADS:] for a in range(3)]
                    run(dve.tensor_tensor(tmp[:, 3, :, :], low[0], low[1], ALU.min))
                    run(dve.tensor_tensor(tmp[:, 3, :, :], tmp[:, 3, :, :], low[2], ALU.min))
                    for a in range(3):
                        ins = dve.tensor_tensor(tmp[:, a, :, :], tmp[:, 3, :, :], low[a], ALU.subtract)
                        tell(ins, dif_lse) if a == 2 else run(ins)
                    dve.wait_ge(exp_lse, 1)
                    for a in range(3):
                        run(dve.tensor_tensor(low[a], tmp[:, a, :, :], lse[a], ALU.mult))
                    run(dve.tensor_tensor(tmp[:, 3, :, :], low[0], low[1], ALU.add))
                    run(dve.tensor_tensor(tmp[:, 3, :, :], tmp[:, 3, :, :], low[2], ALU.add))
                    run(dve.reciprocal(tmp[:, 3, :, :], tmp[:, 3, :, :]))
                    for a in range(3):
                        run(dve.tensor_tensor(tmp[:, a, :, :], tmp[:, a, :, :], tmp[:, 3, :, :], ALU.mult))
                if s + 1 in YA_SLOTS:
                    t = s + 1 - YA_SLOTS[0]
                    parts = [x[:, t, :].rearrange("p (h d) -> p h d", h=HEADS) for x in (On0, On1, O)]
                    for a in range(3):
                        run(dve.tensor_tensor(parts[a], parts[a], tmp[:, a, t, :].unsqueeze(2).to_broadcast([P, HEADS, HD]),
                                              ALU.mult))
                    run(dve.tensor_tensor(O[:, t, :], O[:, t, :], On0[:, t, :], ALU.add))
                    tell(dve.tensor_tensor(O[:, t, :], O[:, t, :], On1[:, t, :], ALU.add), ya_ready)
                if s in YA_SLOTS:
                    t = s - YA_SLOTS[0]
                    dve.wait_ge(ya_hi_done, t + 1)
                    tell(dve.tensor_tensor(ya_lo[:, :, t * P:(t + 1) * P], quarters(7),
                                           ya_hi[:, :, t * P:(t + 1) * P].bitcast(F32), ALU.subtract), ya_split)
                dve_block(s)

            def dve_block(s):
                slab, i = divmod(s, 4)
                src = bank(s % 2)
                if slab == SL_HF:
                    dve.wait_ge(evac["act"], i + 1)
                    run(dve.tensor_scalar(E3[:, :], HF[:, i, :], lb_a[:, i:i + 1], lb_b[:, i:i + 1], ALU.mult, ALU.add))
                    run(dve.tensor_scalar(HK[:, i, :], HF[:, i, :], -1.0, 1.0, ALU.mult, ALU.add))
                    run(dve.tensor_scalar(HK[:, i, :], HK[:, i, :], lb_a[:, i:i + 1], None, ALU.mult))
                    tell(dve.tensor_copy(HF[:, i, :], E3[:, :]), f_ready)
                elif slab == SL_HQ or slab == SL_OG:
                    dve.wait_ge(tanh_ready, i + (1 if slab == SL_HQ else 5))
                    dst = (HQ if slab == SL_HQ else HOG)[:, i, :]
                    tell(dve.scalar_tensor_tensor(dst, dst, 1.0, src, ALU.add, ALU.mult), evac["dve"])
                elif slab == SL_HI:
                    dve.wait_ge(proj_done, s + 1)
                    if i == 0:
                        dve.wait_ge(line_stored, 48)
                    tell(dve.tensor_copy(HV[:, i, :], src), evac["dve"])
                elif evacuator(s) == "dve":
                    a = (slab - SL_ATT) // 3
                    dve.wait_ge(proj_done, s + 1)
                    tell(dve.tensor_copy((VA, VB, VA)[a][:, i, :], src), evac["dve"])

            for s in range(N_SLOTS):
                slot_dve(s)

            for j in range(KC):
                b = 2 + 2 * (j % 2)
                half, i = divmod(j, 4)
                dve.wait_ge(br_done, 2 * j + 1)
                run(dve.scalar_tensor_tensor(m1[:, :], gates[2 * half][:, i, :], 1.0, bank(b), ALU.add, ALU.mult))
                dve.wait_ge(br_done, 2 * j + 2)
                tell(dve.scalar_tensor_tensor(m2[:, :], gates[2 * half + 1][:, i, :], 1.0, bank(b + 1), ALU.add, ALU.mult),
                     br_read)
                tell(dve.tensor_tensor(m1[:, :], m1[:, :], m2[:, :], ALU.add), m_ready)
                dve.wait_ge(m_hi, j + 1)
                tell(dve.scalar_tensor_tensor(mT[:, 1, j, :], m1[:, :], 0.5, mT[:, 0, j, :].bitcast(F32),
                                              ALU.mult, ALU.subtract), m_split)

            def low_h2(t):
                dve.wait_ge(h2_hi_done, t + 1)
                cols = slice(t * P, (t + 1) * P)
                tell(dve.tensor_tensor(h2_lo[:, :, cols], bank(4 + 2 * (t % 2), 2).rearrange("p b (k c) -> p (b k) c", c=P),
                                       h2_hi[:, :, cols].bitcast(F32), ALU.subtract), h2_split)

            dve.wait_ge(x2_landed, 16)
            dve.wait_ge(wn_landed, 32)
            for t in range(NT):
                b = 2 * (t % 2)
                dve.wait_ge(wo_ssq, 2 * t + 1)
                root(ss[:, t:t + 1], DM, 1)
                tell(dve.scalar_tensor_tensor(mixed[:, :], ps[:, b:b + 2, :].rearrange("p b c -> p (b c)"), rstd[:, 0:1],
                                              w_post[:, :], ALU.mult, ALU.mult), wo_read)
                tell(dve.tensor_tensor(x2[:, t, :], x2[:, t, :], mixed[:, :], ALU.add), wo_res)
                dve.wait_ge(wo_ssq, 2 * t + 2)
                root(ss[:, NT + t:NT + t + 1], DM, 1)
                if t:
                    dve.wait_ge(h2t_done, t)
                tell(dve.scalar_tensor_tensor(xn2[:, :], x2[:, t, :], rstd[:, 0:1], w_pre2[:, :], ALU.mult, ALU.mult),
                     xn2_ready)
                if t:
                    low_h2(t - 1)
            low_h2(NT - 1)

            tell(dve.memset(up[0][:, 0:2], 0.0), pads_ready)
            tell(dve.memset(up[1][:, 0:2], 0.0), pads_ready)

            def up_tile(f):
                for half in range(2):
                    c = f + half * FT
                    dve.wait_ge(tap0_done, 2 * f + (half + 1))
                    dve.scalar_tensor_tensor(cv[half][:, :], up[half][:, 1:SEQ + 1], cw[:, 1, bass.ds(c, 1)], cv[half][:, :],
                                             ALU.mult, ALU.add).then_inc(tap1_done, 1)
                    dve.wait_ge(tap1_done, 2 * f + (half + 1))
                    dve.scalar_tensor_tensor(cv[half][:, :], up[half][:, 2:], cw[:, 2, bass.ds(c, 1)], cv[half][:, :],
                                             ALU.mult, ALU.add).then_inc(conv_done, 1)
                dve.wait_ge(conv_done, 2 * f + 2)
                dve.wait_ge(gelu_done, f + 1)
                dve.tensor_tensor(aT[:, bass.ds(f, 1), :].rearrange("p o c -> p (o c)"), ge[:, :], cv[1][:, :],
                                  ALU.mult).then_inc(a_ready, 1)

            for k in range(2):
                up_tile(k)
            with dve.Fori(0, (UPS - 1) // 2) as g:
                for k in range(4):
                    up_tile(4 * g + (2 + k))

            for q in range(2 * FT):
                dve.wait_ge(a_hi_done, q + 1)
                dve.tensor_tensor(a_lo[:, q % 4, :], aT[:, q % FT, :], a_hi[:, q % 4, :].bitcast(F32),
                                  ALU.subtract).then_inc(a_split, 1)
                t = q - FT - 1
                if 0 <= t < NT:
                    dve.wait_ge(down_chunk, FT)
                    tell(dve.tensor_copy(d0[:, t, :], bank(t)), d0_ready)
            dve.wait_ge(wf_landed, 16)
            dve.wait_ge(a_split, 2 * FT)
            for t in range(NT):
                dve.wait_ge(fin_ssq, NT + t + 1)
                root(ss[:, t:t + 1], DM, 1, extra=ss[:, NT + t:NT + t + 1])
                if t >= 2:
                    dve.wait_ge(out_stored[t % 2], 16)
                r = res[t % 2]
                run(dve.scalar_tensor_tensor(r[:, 0:COLS], d0[:, t, :], rstd[:, 0:1], w_ffn[:, 0:COLS], ALU.mult, ALU.mult))
                run(dve.scalar_tensor_tensor(r[:, COLS:], bank(4 + t), rstd[:, 0:1], w_ffn[:, COLS:], ALU.mult, ALU.mult))
                tell(dve.tensor_tensor(r[:, :], r[:, :], x2[:, t, :], ALU.add), out_ready)

        @block.tensor
        def _(pe):
            def three(dst, pairs, after=None):
                last = len(pairs) - 1
                for n, (w, m) in enumerate(pairs):
                    if after and n in after:
                        after[n]()
                    pe.matmul(dst, w[0], m[0], start=n == 0, stop=False)
                    pe.matmul(dst, w[0], m[1], start=False, stop=False)
                    ins = pe.matmul(dst, w[1], m[0], start=False, stop=n == last)
                return ins

            def w_cols(n0, k, c0=0, width=COLS):
                w = split_place(n0 + k // 2)
                return tuple(ws[:, w, part, k % 2, c0:c0 + width] for part in range(2))

            def tokens(k, t, d):
                out = []
                for part in range(2):
                    row = hT[:, part, k, :]
                    out.append(row[:, t * P:(t + 1) * P] if d == 1 else row.rearrange("p (u r) -> p r u", r=d)[:, t, :])
                return tuple(out)

            def project(s, middle):
                slab, i = divmod(s, 4)
                if i == 0:
                    pe.wait_ge(lo_done, 4 * (slab + 1))
                if s >= 2:
                    pe.wait_ge(evac[evacuator(s - 2)], evacuated(s - 2))
                by_token = slab in (SL_HI, SL_OG) or (SL_ATT <= slab < SL_GATE and (slab - SL_ATT) % 3 == 0)
                if by_token:
                    d = STRIDE[GROUPS[(slab - SL_ATT) // 3]] if slab >= SL_ATT else 1
                    pairs = [(tokens(k, i, d), w_cols(4 * slab, k)) for k in range(KC)]
                else:
                    pairs = [(w_cols(4 * slab, k, i * P, P), (hT[:, 0, k, :], hT[:, 1, k, :])) for k in range(KC)]
                three(bank(s % 2), pairs, {KC // 2: middle}).then_inc(proj_done, 1)

            pe.wait_ge(rel_landed, 48)
            for g in range(3):
                pe.matmul(ps[0:HEADS, (6, 7, 0)[g], 0:LINE], rel[:, g * HEADS:(g + 1) * HEADS], onehot[:, g, :],
                          start=True, stop=True).then_inc(line_done, 1)
            pe.wait_ge(const_landed, 32)
            for t in range(NT):
                pe.wait_ge(xn_ready, t + 1)
                if t >= 2:
                    pe.wait_ge(hT_ready, t - 1)
                for k in range(KC):
                    ins = pe.transpose(quarters(2 + 2 * (t % 2) + k // 4)[:, k % 4, :], xn[:, t % 2, k * P:(k + 1) * P],
                                       ident[:, :])
                ins.then_inc(xt_done, 1)
            pe.wait_ge(hT_ready, NT)
            pe.wait_ge(line_ready, 3)

            def scores(a, h):
                idx = HEADS * a + h
                r = slice(HD * (h % 2), HD * (h % 2) + HD)
                j = h // 2
                if idx == 0:
                    pe.wait_ge(o_read, NT)
                    pe.wait_ge(yh_split, NT)
                else:
                    pe.wait_ge(exp_done, idx)
                if h == 0:
                    pe.wait_ge(evac["act"], evacuated(4 * (SL_ATT + 3 * a + 2) + 3))
                for n in range(NT):
                    q = QT[r, j, n * P:(n + 1) * P]
                    if a < 2:
                        ins = pe.matmul(quarters(2)[:, n, :], q, KT[r, j, n * P:(n + 1) * P], start=True, stop=True)
                    elif n == 0:
                        ins = pe.matmul(scores2[:, 0, P:], q, KT[r, j, 0:P], start=True, stop=True)
                    else:
                        ins = pe.matmul(scores2[:, n, :], q, KT[r, j, (n - 1) * P:(n + 1) * P], start=True, stop=True)
                ins.then_inc(scores_done, 1)

            def transpose_probs(a, h):
                idx = HEADS * a + h
                pe.wait_ge(exp_done, idx + 1)
                if idx:
                    pe.wait_ge(pt_ready, idx)
                else:
                    pe.wait_ge(chain_done, HH * NT)
                for n in range(NT):
                    ins = pe.transpose(pt_banks[:, n, :], PR[:, idx % 2, n, P:], ident[:, :])
                if a == 2:
                    for n in range(1, NT):
                        ins = pe.transpose(pt_banks[:, 3 + n, :], PR[:, idx % 2, n, 0:P], ident[:, :])
                ins.then_inc(pt_done, 1)

            def weigh_values(a, h):
                idx = HEADS * a + h
                pe.wait_ge(pt_ready, idx + 1)
                if idx:
                    pe.wait_ge(o_saved, idx)
                V = (VA, VB, VA)[a]
                cols = slice(h * HD, (h + 1) * HD)
                for n in range(NT):
                    dst = ps[:, 6, n * HD:(n + 1) * HD]
                    if a == 2 and n:
                        pe.matmul(dst, PT[:, 3 + n, :], V[:, n - 1, cols], start=True, stop=False)
                    ins = pe.matmul(dst, PT[:, n, :], V[:, n, cols], start=not (a == 2 and n), stop=True)
                ins.then_inc(pv_done, 1)

            def recur_first(t):
                cols = slice(t * P, (t + 1) * P)
                if t == 0:
                    pe.wait_ge(prep_done, HH)
                    pe.wait_ge(evac["dve"], 2 * 4)
                else:
                    pe.wait_ge(o_read, t)
                for h in range(HH):
                    ins = pe.matmul(quarters(2)[:, h, :], HKX[:, h, cols], HQ[:, h, cols], start=True, stop=True)
                ins.then_inc(at_done, 1)
                if t >= 2:
                    pe.wait_ge(yh_split, t - 1)
                for h in range(HH):
                    ins = pe.transpose(quarters(3)[:, h, :], HK[:, h, cols], ident[:, :])
                ins.then_inc(kdt_done, 1)

            def recur_kv(t):
                pe.wait_ge(kd_ready, t + 1)
                if t:
                    pe.wait_ge(chain_done, HH * t)
                for h in range(HH):
                    for c in range(4):
                        rows = slice(CH * c, CH * (c + 1))
                        ins = pe.matmul(quarters(4 + c)[:, h, :], kd[rows, h, :], HV[rows, t, h * P:(h + 1) * P],
                                        start=True, stop=True)
                ins.then_inc(kv_done, 1)

            def recur_out(t, h):
                pe.wait_ge(at_ready, t + 1)
                pe.wait_ge(chain_done, HH * t + h + 1)
                pe.matmul(quarters(2)[:, h, :], AT[:, h, :], HV[:, t, h * P:(h + 1) * P], start=True, stop=False,
                          skip_group_check=True)
                for c in range(4):
                    state = carry[:, t % 2, h, :] if c == 0 else states[:, h, c - 1, :]
                    q = HQ[:, h, t * P + CH * c:t * P + CH * (c + 1)]
                    ins = pe.matmul(quarters(2)[CH * c:CH * (c + 1), h, :], q, state, start=False, stop=True,
                                    skip_group_check=True)
                ins.then_inc(o_done, 1)

            for s in range(N_SLOTS):
                if attn_at(s):
                    scores(*attn_at(s))
                for t in range(NT):
                    if s == group_slot(t):
                        recur_first(t)
                    if s == group_slot(t) + 2:
                        recur_out(t, 2)
                        recur_out(t, 3)

                def middle(s=s):
                    if s >= 1 and attn_at(s - 1):
                        transpose_probs(*attn_at(s - 1))
                    for t in range(NT):
                        if s == group_slot(t):
                            recur_kv(t)
                        if s == group_slot(t) + 1:
                            recur_out(t, 0)
                            recur_out(t, 1)
                    for t in range(NT):
                        if s == group_slot(t) + 3:
                            pe.wait_ge(yo_ready, t + 1)
                            if t + 1 < NT:
                                pe.wait_ge(kd_ready, t + 2)
                            for h in range(HH):
                                ins = pe.transpose(quarters(3)[:, h, :], yo[:, h, :], ident[:, :])
                            ins.then_inc(yht_done, 1)
                    if s in YA_SLOTS:
                        t = s - YA_SLOTS[0]
                        pe.wait_ge(ya_ready, t + 1)
                        if t:
                            pe.wait_ge(ya_split, t)
                        for c in range(4):
                            ins = pe.transpose(quarters(7)[:, c, :], O[:, t, c * P:(c + 1) * P], ident[:, :])
                        ins.then_inc(yat_done, 1)

                project(s, middle)
                if s >= 1 and attn_at(s - 1):
                    weigh_values(*attn_at(s - 1))

            pe.wait_ge(ya_split, NT)
            for j in range(KC):
                half, i = divmod(j, 4)
                slab = SL_BR + half
                if i == 0:
                    pe.wait_ge(lo_done, 4 * (slab + 1))
                if j >= 2:
                    pe.wait_ge(br_read, j - 1)
                for part, y in enumerate(((ya_hi, ya_lo), (yh_hi, yh_lo))):
                    three(bank(2 + 2 * (j % 2) + part),
                          [(w_cols(4 * slab, 4 * part + k, i * P, P), (y[0][:, k, :], y[1][:, k, :])) for k in range(4)]
                          ).then_inc(br_done, 1)

            def transpose_h2(t):
                pe.wait_ge(xn2_ready, t + 1)
                if t >= 2:
                    pe.wait_ge(h2_split, t - 1)
                for k in range(KC):
                    ins = pe.transpose(quarters(4 + 2 * (t % 2) + k // 4)[:, k % 4, :], xn2[:, k * P:(k + 1) * P], ident[:, :])
                ins.then_inc(h2t_done, 1)

            pe.wait_ge(m_split, KC)
            pe.wait_ge(evac["act"], evacuated(N_SLOTS - 1))
            for n, (t, half) in enumerate(WO_ORDER):
                slab = SL_WO + half
                pe.wait_ge(lo_done, 4 * (slab + 1))
                if t >= 2:
                    pe.wait_ge(wo_read, t - 1)
                three(bank(2 * (t % 2) + half),
                      [(tuple(mT[:, part, k, t * P:(t + 1) * P] for part in range(2)), w_cols(4 * slab, k))
                       for k in range(KC)]).then_inc(wo_done, 1)
                if n >= 5:
                    transpose_h2(n - 5)
            transpose_h2(NT - 1)

            def up_tile(f, k, place0, bank0):
                for half in range(2):
                    if not isinstance(f, int) or f >= 2:
                        pe.wait_ge(up_copied, 2 * f + (half - 3))
                    pairs = []
                    for c in range(KC):
                        cols = slice(256 * half + k * P, 256 * half + (k + 1) * P)
                        w = place0 + c // 2
                        pairs.append(((ws[:, w, 0, c % 2, cols], ws[:, w, 1, c % 2, cols]), (h2_hi[:, c, :], h2_lo[:, c, :])))
                    three(bank(bank0 + half), pairs).then_inc(up_done, 1)

            pe.wait_ge(h2_split, NT)
            pe.wait_ge(wo_read, NT)
            pe.wait_ge(lo_done, PAIRS_UP + 4)
            for k in range(2):
                up_tile(k, k, split_place(PAIRS_UP), 2 * k)
            with pe.Fori(0, (UPS - 1) // 2) as g:
                for u in range(2):
                    pe.wait_ge(lo_done, 8 * g + (PAIRS_UP + 4 * (u + 2)))
                    for k in range(2):
                        up_tile(4 * g + (2 + 2 * u + k), k, split_place(PAIRS_UP + 4 * (u + 1)), 2 * k)

            def down(half, q, t, last=False):
                w = split_place(PAIRS_DOWN + q // 2)
                k = q % FT
                pairs = [(tuple(x[:, q % 4, t * P:(t + 1) * P] for x in (a_hi, a_lo)),
                          (ws[:, w, 0, q % 2, :], ws[:, w, 1, q % 2, :]))]
                (w0, w1), (r0, r1) = pairs[0]
                dst = bank(4 * half + t)
                pe.matmul(dst, w0, r0, start=k == 0, stop=False)
                pe.matmul(dst, w0, r1, start=False, stop=False)
                return pe.matmul(dst, w1, r0, start=False, stop=k == FT - 1)

            pe.wait_ge(up_copied, 2 * FT)
            for q in range(2 * FT - 4):
                half = q // FT
                pe.wait_ge(a_split, q + 1)
                pe.wait_ge(lo_done, PAIRS_DOWN + q // 2 + 1)
                for t in range(NT):
                    ins = down(half, q, t)
                ins.then_inc(down_chunk, 1)
            pe.wait_ge(a_split, 2 * FT)
            pe.wait_ge(lo_done, N_PAIRS)
            for t in range(NT):
                for q in range(2 * FT - 4, 2 * FT):
                    ins = down(1, q, t)
                ins.then_inc(down_tile, 1)


def bucket(dist):
    n = np.maximum(dist, 0)
    nf = np.maximum(n, 1).astype(np.float32)
    large = 16 + (np.log(nf / np.float32(16)) / np.float32(math.log(2048 / 16)) * np.float32(16)).astype(np.int32)
    return np.where(n < 16, n, np.minimum(large, 31))


def constants():
    x = np.arange(LINE)
    dist = 2 * P - 1 - x
    ok = (dist >= 0) & (dist <= P)
    onehot = np.zeros((32, 3, LINE), np.float32)
    line_add = np.full((HEADS, 3, LINE), NEG, np.float32)
    for g, (d, stride) in enumerate(zip(DILATION, STRIDE)):
        b = bucket(dist * stride)
        use = ok & (dist % (d // stride) == 0)
        onehot[b[use], g, x[use]] = 1.0
        line_add[:, g, use] = 0.0
    j, i = np.arange(P)[:, None], np.arange(P)[None, :]
    return {
        "onehot": onehot,
        "line_add": line_add,
        "ident": np.eye(P, dtype=np.float32),
        "chunk_mask": ((j // CH == i // CH) & (j <= i)).astype(np.float32),
        "scan_mask": np.broadcast_to((np.arange(SEQ) % CH != 0).astype(np.float32), (P, SEQ)),
    }


def stream(w_in, w_branch_attn, w_branch_hgrn, w_out, w_up, w_down):
    attn, hg, gate = 4608, 4608, 4608 + 2048
    qkv = lambda g, which: w_in[:, (3 * g + which) * COLS:(3 * g + which + 1) * COLS]
    hcol = lambda n: w_in[:, hg + n * COLS:hg + (n + 1) * COLS]
    slabs = [hcol(1), hcol(0), hcol(2), hcol(3)]
    for g in GROUPS:
        slabs += [qkv(g, 2), qkv(g, 0), qkv(g, 1)]
    for half in range(2):
        for b in range(2):
            at = gate + b * DM + half * COLS
            slabs.append(w_in[:, at:at + COLS])
    for half in range(2):
        c = slice(half * COLS, (half + 1) * COLS)
        slabs.append(np.concatenate([w_branch_attn[:, c], w_branch_hgrn[:, c]], 0))
    for half in range(2):
        slabs.append(w_out[:, half * COLS:(half + 1) * COLS])
    for u in range(UPS):
        slabs.append(np.concatenate([w_up[:, 256 * u:256 * (u + 1)], w_up[:, DFF + 256 * u:DFF + 256 * (u + 1)]], 1))
    rows = np.concatenate(slabs + [w_down[:, 0:COLS], w_down[:, COLS:]], 0)
    return np.ascontiguousarray(rows.reshape(N_PAIRS, 2, P, COLS).transpose(0, 2, 1, 3))


def kernel(x, pre_mix_norm, w_in, rel_bias, hgrn_lb_raw, hgrn_norm, w_branch_attn, w_branch_hgrn, w_out,
           post_mix_norm, pre_ffn_norm, w_up, conv_w, conv_b, w_down, post_ffn_norm):
    import concourse.bacc as bacc
    from concourse.bass_utils import run_bass_kernel_spmd

    arrays = {
        "x": x[0],
        "stream": stream(*(np.asarray(w)[0] for w in (w_in, w_branch_attn, w_branch_hgrn, w_out, w_up, w_down))),
        "pre_mix": pre_mix_norm[0], "post_mix": post_mix_norm[0], "pre_ffn": pre_ffn_norm[0], "post_ffn": post_ffn_norm[0],
        "rel_bias": rel_bias,
        "lb_raw": np.asarray(hgrn_lb_raw).reshape(2, HH, P).transpose(2, 0, 1),
        "hgrn_norm": hgrn_norm[0],
        "conv": np.concatenate([conv_w[0], conv_b], 0).reshape(4, 2 * FT, P).transpose(2, 0, 1),
        **constants(),
    }
    nc = bacc.Bacc("TRN2", target_bir_lowering=False, num_devices=1)
    fed, A = {}, {}
    for name, a in arrays.items():
        a = np.ascontiguousarray(a)
        fed[f"in_{name}"] = a
        A[name] = nc.dram_tensor(f"in_{name}", a.shape, mybir.dt.from_np(a.dtype), kind="ExternalInput").ap()
    A["table_scratch"] = [nc.dram_tensor(f"table_scratch{a}", (P, HEADS, P if a < 2 else 2 * P), F32, kind="Internal").ap()
                          for a in range(3)]
    for name, shape in (("O_scratch", (2, SEQ, COLS)), ("stat_scratch", (2, SEQ, 2 * HEADS))):
        A[name] = nc.dram_tensor(name, shape, F32, kind="Internal").ap()
    A["out"] = nc.dram_tensor("out", (SEQ, DM), F32, kind="ExternalOutput").ap()
    build(nc, A)
    got = run_bass_kernel_spmd(nc, [fed], core_ids=[0]).results[0]["out"]
    return got.reshape(1, SEQ, DM)
```

```python
import math
from contextlib import ExitStack

import numpy as np

import concourse.bass as bass
from concourse import mybir

F32 = mybir.dt.float32
F32R = mybir.dt.float32r
U8 = mybir.dt.uint8
ALU = mybir.AluOpType
ACT = mybir.ActivationFunctionType
AX_X = mybir.AxisListType.X

P = 128
SEQ, DM = 512, 1024
NT = SEQ // P
KC = DM // P
COLS = 512
HEADS, HD = 8, 64
HH = 4
CH = 32
DFF = 2816
FT = DFF // P
UPS = DFF // 256
EPS = 1e-6
NEG = -1e30
GROUPS = (1, 2, 0)
DILATION = (1, 4, 16)
STRIDE = (1, 4, 4)
LINE = 3 * P

SL_HI, SL_HF, SL_HQ, SL_OG = 0, 1, 2, 3
SL_ATT = 4
SL_GATE = SL_ATT + 9
SL_BR = SL_GATE + 4
SL_WO = SL_BR + 2
SL_UP = SL_WO + 2
N_SLOTS = 4 * SL_BR
PAIRS_UP = 4 * SL_UP
PAIRS_DOWN = PAIRS_UP + 4 * UPS
N_PAIRS = PAIRS_DOWN + FT
RAW = 4
RING = 8
UP0_PLACE = 17
DOWN_RING = (0, 1, 2, 3, 4, 5, 6, 7, 12, 13, 8)
A_RING = 5


def head_slot(a, h):
    return 4 * (SL_ATT + 3 * a + 3) + h


def group_slot(t):
    return 4 * SL_OG + 1 + 3 * t


YA_SLOTS = range(N_SLOTS - NT, N_SLOTS)


def attn_at(s):
    for a in range(3):
        if 0 <= s - head_slot(a, 0) < HEADS:
            return a, s - head_slot(a, 0)
    return None


def evacuator(s):
    slab = s // 4
    if slab == SL_HF or slab >= SL_GATE:
        return "act"
    if slab < SL_ATT:
        return "dve"
    return "dve" if (slab - SL_ATT) % 3 == 0 else "act"


def evacuated(s):
    return sum(evacuator(i) == evacuator(s) for i in range(s + 1))


def build(nc, A):
    ctx = ExitStack()
    with ctx:
        base = 16512
        top = [base]

        def place(name, shape, dt, at=None):
            size = int(np.prod(shape[1:])) * (1 if dt == U8 else 4)
            if at is None:
                at = top[0]
                top[0] = at + (size + 31) // 32 * 32
                assert top[0] <= 229368, (name, top[0])
            return nc.alloc_sbuf_tensor_at(name, shape, dt, offset=at)

        def sem(name):
            return ctx.enter_context(nc.semaphore(name))

        KB = 1024
        raw = place("raw", [P, RAW, 2, COLS], F32)
        ws_at = top[0]
        ws = place("ws", [P, UP0_PLACE + 4, 2, 2, COLS], F32R, ws_at)
        top[0] = ws_at + 12 * 8 * KB
        hT = place("hT", [P, 2, KC, SEQ], F32R, ws_at + RING * 8 * KB)
        mT = place("mT", [P, 2, KC, SEQ], F32R, ws_at + RING * 8 * KB)
        ar = top[0]
        top[0] = ar + 92 * KB
        HF = place("HF", [P, HH, SEQ], F32, ar)
        HK = place("HK", [P, HH, SEQ], F32, ar + 8 * KB)
        HQ = place("HQ", [P, HH, SEQ], F32, ar + 16 * KB)
        HKX = place("HKX", [P, HH, SEQ], F32, ar + 24 * KB)
        HV = place("HV", [P, NT, COLS], F32, ar + 32 * KB)
        HOG = place("HOG", [P, NT, COLS], F32, ar + 40 * KB)
        scan_mask = place("scan_mask", [P, SEQ], F32, ar + 56 * KB)
        E1, E2, E3 = [place(name, [P, 2, SEQ], F32, ar + at * KB) for name, at in (("E1", 58), ("E2", 62), ("E3", 66))]
        mask_f = place("mask_f", [P, P], F32, ar + 72 * KB)
        carry = place("carry", [P, 2, HH, P], F32, ar + 56 * KB)
        states = place("states", [P, HH, 3, P], F32, ar + 60 * KB)
        AT = place("AT", [P, HH, P], F32, ar + 84 * KB)
        kd = place("kd", [P, HH, P], F32, ar + 86 * KB)
        yo = place("yo", [P, HH, P], F32, ar + 88 * KB)
        junk_h = place("junk_h", [P, P], F32, ar + 90 * KB)
        yh_hi = place("yh_hi", [P, HH, SEQ], F32R, ar + 68 * KB)
        yh_lo = place("yh_lo", [P, HH, SEQ], F32R, ar + 76 * KB)
        QT = place("QT", [P, 4, SEQ], F32, ar)
        KT = place("KT", [P, 4, SEQ], F32, ar + 8 * KB)
        bias_a = place("bias_a", [P, HEADS, P], F32, ar + 16 * KB)
        bias_b = place("bias_b", [P, HEADS, P], F32, ar + 20 * KB)
        bias_c = place("bias_c", [P, HEADS, 2 * P], F32, ar + 16 * KB)
        O = place("O", [P, NT, COLS], F32, ar + 24 * KB)
        PR = place("PR", [P, 2, NT, 2 * P], F32, ar + 32 * KB)
        VB = place("VB", [P, NT, COLS], F32, ar + 40 * KB)
        VA = place("VA", [P, NT, COLS], F32, ar + 48 * KB)
        PT = place("PT", [P, 8, P], F32, ar + 56 * KB)
        On0 = place("On0", [P, NT, COLS], F32, ar + 40 * KB)
        On1 = place("On1", [P, NT, COLS], F32, ar + 32 * KB)
        ya_hi = place("ya_hi", [P, 4, SEQ], F32R, ar + 16 * KB)
        ya_lo = place("ya_lo", [P, 4, SEQ], F32R, ar + 48 * KB)
        gates = [place("gate0a", [P, 4, SEQ], F32, ar + 60 * KB), place("gate1a", [P, 4, SEQ], F32, ar + 84 * KB),
                 place("gate0b", [P, 4, SEQ], F32, ar), place("gate1b", [P, 4, SEQ], F32, ar + 8 * KB)]
        m1 = place("m1", [P, SEQ], F32, ar + 56 * KB)
        m2 = place("m2", [P, SEQ], F32, ar + 58 * KB)
        x_in = place("x_in", [P, NT, DM], F32, ar)
        w_pre = place("w_pre", [P, DM], F32, ar + 16 * KB)
        xn = place("xn", [P, 2, DM], F32, ar + 20 * KB)
        onehot = place("onehot", [32, 3, LINE], F32, ar + 40 * KB)
        line_add = place("line_add", [HEADS, 3, LINE], F32, ar + 45 * KB)
        lines = place("lines", [HEADS, 3, LINE], F32, ar + 50 * KB)
        rel = place("rel", [32, 3 * HEADS], F32, ar + 55 * KB)
        junk_x = place("junk_x", [P, DM], F32, ar + 68 * KB)
        x2 = place("x2", [P, NT, DM], F32, ar + 76 * KB)
        h2_hi = place("h2_hi", [P, KC, SEQ], F32R, ar)
        h2_lo = place("h2_lo", [P, KC, SEQ], F32R, ar + 16 * KB)
        w_post = place("w_post", [P, DM], F32, ar + 32 * KB)
        w_pre2 = place("w_pre2", [P, DM], F32, ar + 72 * KB)
        mixed = place("mixed", [P, DM], F32, ar + 36 * KB)
        aT = place("aT", [P, FT, SEQ], F32, ar + 32 * KB)
        conv_at = ws_at + RING * 8 * KB
        up = [place("up_gate", [P, SEQ + 2], F32, conv_at), place("up_val", [P, SEQ + 2], F32, conv_at + 2080)]
        cv = [place("cv_gate", [P, SEQ], F32, conv_at + 5 * KB), place("cv_val", [P, SEQ], F32, conv_at + 7 * KB)]
        ge = place("ge", [P, SEQ], F32, conv_at + 9 * KB)
        a_hi = place("a_hi", [P, A_RING, SEQ], F32R, ws_at + 76 * KB)
        a_lo = place("a_lo", [P, A_RING, SEQ], F32R, ws_at + 86 * KB)
        d0 = place("d0", [P, NT, COLS], F32, ar + 16 * KB)
        w_ffn = place("w_ffn", [P, DM], F32, ar + 24 * KB)
        res = [place("res0", [P, DM], F32, ar + 28 * KB), place("res1", [P, DM], F32, ar + 32 * KB)]
        junk_d = place("junk_d", [P, COLS], F32, ar + 36 * KB)
        ident = place("ident", [P, P], F32)
        h_norm = place("h_norm", [P, P], F32)
        chunk_mask = place("chunk_mask", [P, P], U8)
        cw = place("cw", [P, 4, 2 * FT], F32)
        stat = place("stat", [P, 3, NT, 2 * HEADS], F32)
        tmp = place("tmp", [P, 4, NT, HEADS], F32)
        chunk_decay = place("chunk_decay", [P, HH, SEQ // CH], F32)
        lb = place("lb", [P, 2, HH], F32)
        lb_a = place("lb_a", [P, HH], F32)
        lb_b = place("lb_b", [P, HH], F32)
        ss = place("ss", [P, 8], F32)
        var = place("var", [P, 4], F32)
        var0 = place("var0", [P, NT], F32)
        rstd = place("rstd", [P, 4], F32)
        minus_half = place("minus_half", [P, 4], F32)
        mx = place("mx", [P, 4], F32)

        ps = ctx.enter_context(nc.psum_tensor("ps", [P, 8, COLS], F32))

        def bank(b, n=1):
            return ps[:, b, :] if n == 1 else ps[:, b:b + n, :]

        def quarters(b):
            return ps[:, b, :].rearrange("p (q c) -> p q c", q=4)

        pt_banks = ps[:, 4:6, :].rearrange("p b (n k) -> p (b n) k", n=4)
        scores2 = ps[:, 2:4, :].rearrange("p b (n k) -> p (b n) k", n=2)

        def low_hT(t, tell):
            cols = slice(t * P, (t + 1) * P)
            tell(nc.vector.tensor_tensor(hT[:, 1, :, cols], bank(2 + 2 * (t % 2), 2).rearrange("p b (k c) -> p (b k) c", c=P),
                                         hT[:, 0, :, cols].bitcast(F32), ALU.subtract), hT_ready)

        raw_landed = [sem(f"raw_landed{i}") for i in range(RAW)]
        hi_done, lo_done = sem("hi_done"), sem("lo_done")
        x_landed = [sem(f"x_landed{i}") for i in range(NT)]
        w_pre_landed, ident_landed = sem("w_pre_landed"), sem("ident_landed")
        lb_landed, rel_landed = sem("lb_landed"), sem("rel_landed")
        lb_dif, lb_tanh = sem("lb_dif"), sem("lb_tanh")
        act_step, dve_step, pool_step = sem("act_step"), sem("dve_step"), sem("pool_step")
        line_done, line_ready, line_stored = sem("line_done"), sem("line_ready"), sem("line_stored")
        ssq_ready, var_ready, rstd_ready = sem("ssq_ready"), sem("var_ready"), sem("rstd_ready")
        xn_ready, xt_done, hT_hi, hT_ready = sem("xn_ready"), sem("xt_done"), sem("hT_hi"), sem("hT_ready")
        proj_done, evac = sem("proj_done"), {"act": sem("proj_free_act"), "dve": sem("proj_free_dve")}
        tanh_ready, f_ready, log_ready = sem("tanh_ready"), sem("f_ready"), sem("log_ready")
        G_ready, exp_G, dif_ready, exps_ready, prep_done = sem("G_ready"), sem("exp_G"), sem("dif_ready"), sem("exps_ready"), sem("prep_done")
        at_done, at_ready, kdt_done, kd_ready = sem("at_done"), sem("at_ready"), sem("kdt_done"), sem("kd_ready")
        kv_done, chain_done, o_done, o_read = sem("kv_done"), sem("chain_done"), sem("o_done"), sem("o_read")
        yo_ready, yht_done, yh_hi_done, yh_split = sem("yo_ready"), sem("yht_done"), sem("yh_hi_done"), sem("yh_split")
        bias_landed = [sem(f"bias_landed{a}") for a in range(3)]
        scores_done, max_ready, exp_done = sem("scores_done"), sem("max_ready"), sem("exp_done")
        pt_done, pt_ready, pv_done, o_saved = sem("pt_done"), sem("pt_ready"), sem("pv_done"), sem("o_saved")
        O_stored, On_landed = [sem(f"O_stored{a}") for a in range(2)], [sem(f"On_landed{a}") for a in range(2)]
        dif_lse, exp_lse = sem("dif_lse"), sem("exp_lse")
        ya_ready, yat_done, ya_hi_done, ya_split = sem("ya_ready"), sem("yat_done"), sem("ya_hi_done"), sem("ya_split")
        br_done, br_read, m_ready, m_hi, m_split = sem("br_done"), sem("br_read"), sem("m_ready"), sem("m_hi"), sem("m_split")
        x2_landed = [sem(f"x2_landed{t}") for t in range(NT)]
        w_post_landed, w_pre2_landed = sem("w_post_landed"), sem("w_pre2_landed")
        wo_done, wo_ssq, wo_read, wo_res = sem("wo_done"), sem("wo_ssq"), sem("wo_read"), sem("wo_res")
        xn2_ready, h2t_done, h2_hi_done, h2_split = sem("xn2_ready"), sem("h2t_done"), sem("h2_hi_done"), sem("h2_split")
        up_done, up_copied, tap0_done, conv_done, gelu_done, a_ready = (
            sem("up_done"), sem("up_copied"), sem("tap0_done"), sem("conv_done"), sem("gelu_done"), sem("a_ready"))
        pads_ready, tap1_done = sem("pads_ready"), sem("tap1_done")
        a_hi_done, a_split, down_chunk, down_tile = sem("a_hi_done"), sem("a_split"), sem("down_chunk"), sem("down_tile")
        d0_ready, fin_ssq, out_ready, out_stored, wf_landed = (
            sem("d0_ready"), sem("fin_ssq"), sem("out_ready"), [sem(f"out_stored{i}") for i in range(2)], sem("wf_landed"))

        block = ctx.enter_context(nc.Block())

        def teller(eng, step):
            told = {}

            def tell(ins, s):
                ins.then_inc(s, 1)
                told[id(s)] = told.get(id(s), 0) + 1
                eng.wait_ge(s, told[id(s)])

            return (lambda ins: tell(ins, step)), tell

        @block.sync
        def _(sp):
            def load(n, r):
                sp.dma_start(raw[:, r, :, :], A["stream"][n, :, :, :]).then_inc(raw_landed[r], 16)

            def load_x(t):
                sp.dma_start(x_in[:, t, :], A["x"][t * P:(t + 1) * P, :]).then_inc(x_landed[t], 16)

            load_x(0)
            load(0, 0)
            load(1, 1)
            load_x(1)
            load(2, 2)
            load_x(2)
            load(3, 3)
            load_x(3)
            with sp.Fori(1, N_PAIRS // RAW) as g:
                for r in range(RAW):
                    sp.wait_ge(hi_done, RAW * g + (r + 1 - RAW))
                    sp.wait_ge(lo_done, RAW * g + (r + 1 - RAW))
                    load(RAW * g + r, r)
            for n in range(N_PAIRS // RAW * RAW, N_PAIRS):
                sp.wait_ge(hi_done, n - RAW + 1)
                sp.wait_ge(lo_done, n - RAW + 1)
                load(n, n % RAW)
            for t in range(NT):
                for half in range(2):
                    cols = slice(half * COLS, (half + 1) * COLS)
                    sp.wait_ge(out_ready, 2 * t + half + 1)
                    sp.dma_start(A["out"][t * P:(t + 1) * P, cols], res[t % 2][:, cols]).then_inc(out_stored[t % 2], 16)
            for r in range(2):
                sp.wait_ge(out_stored[r], 16 * NT)

        def split_place(n):
            if n >= PAIRS_DOWN:
                return DOWN_RING[(n - PAIRS_DOWN) % len(DOWN_RING)]
            return UP0_PLACE + n - PAIRS_UP if PAIRS_UP <= n < PAIRS_UP + 4 else n % RING

        @block.gpsimd
        def _(pool):
            roots = [0]

            def low(n):
                pool.wait_ge(hi_done, n + 1)
                w = split_place(n)
                pool.tensor_tensor(ws[:, w, 1, :, :], raw[:, n % RAW, :, :], ws[:, w, 0, :, :].bitcast(F32),
                                   ALU.subtract).then_inc(lo_done, 1)

            def root(n):
                roots[0] += 1
                pool.wait_ge(var_ready, roots[0])
                pool.tensor_tensor(rstd[:, 0:n], var[:, 0:n], minus_half[:, 0:n], ALU.pow).then_inc(rstd_ready, 1)

            pool.memset(minus_half[:, :], -0.5).then_inc(pool_step, 1)
            pool.wait_ge(pool_step, 1)
            root(1)
            low(0)
            low(1)
            root(1)
            low(2)
            low(3)
            for s in range(N_SLOTS):
                if s < 2:
                    root(1)
                low(4 + s)
                for t in range(NT):
                    if s == group_slot(t) + 2:
                        root(HH)
            for n in range(N_SLOTS + 4, PAIRS_UP):
                low(n)
            for t in range(NT):
                low(PAIRS_UP + t)
                root(1)
                root(1)
            first = PAIRS_UP + 4
            with pool.Fori(0, (UPS - 1) // 2) as g:
                for r in range(RING):
                    q = first + r
                    pool.wait_ge(hi_done, RING * g + (q + 1))
                    w = split_place(q)
                    pool.tensor_tensor(ws[:, w, 1, :, :], raw[:, q % RAW, :, :],
                                       ws[:, w, 0, :, :].bitcast(F32), ALU.subtract).then_inc(lo_done, 1)
            for n in range(PAIRS_DOWN, N_PAIRS):
                low(n)
            for t in range(NT):
                root(1)

        @block.scalar
        def _(act):
            run, tell = teller(act, act_step)

            def hi(n):
                act.wait_ge(raw_landed[n % RAW], 16 * (n // RAW + 1))
                m = n - PAIRS_DOWN
                before = n // 4 - 2
                if before < 0:
                    pass
                elif before < SL_BR:
                    act.wait_ge(proj_done, 4 * (before + 1))
                elif n < PAIRS_UP:
                    act.wait_ge(br_done, KC * (before - SL_BR + 1) - (1 if n % 4 < 2 else 0))
                elif n < PAIRS_UP + 4:
                    act.wait_ge(m_split, KC)
                elif n < PAIRS_UP + 12:
                    act.wait_ge(wo_done, 2 * NT)
                elif m < 4:
                    act.wait_ge(up_done, 4 * (before - SL_UP + 1))
                elif m < 10:
                    act.wait_ge(up_done, 4 * UPS)
                elif m < len(DOWN_RING):
                    act.wait_ge(a_ready, FT)
                else:
                    act.wait_ge(down_chunk, 2 * (m - len(DOWN_RING) + 1))
                tell(act.activation(ws[:, split_place(n), 0, :, :], raw[:, n % RAW, :, :], ACT.Copy), hi_done)

            act.dma_start(w_pre[:, :], A["pre_mix"].partition_broadcast(P)).then_inc(w_pre_landed, 16)
            act.dma_start(ident[:, :], A["ident"]).then_inc(ident_landed, 16)

            def ssq_x(t):
                act.wait_ge(x_landed[t], 16)
                tell(act.activation(junk_x[:, :], x_in[:, t, :], ACT.Square, accum_out=ss[:, t:t + 1]), ssq_ready)

            def high_hT(t):
                act.wait_ge(xt_done, t + 1)
                b = 2 + 2 * (t % 2)
                tell(act.activation(hT[:, 0, :, t * P:(t + 1) * P],
                                    bank(b, 2).rearrange("p b (k c) -> p (b k) c", c=P), ACT.Copy), hT_hi)

            ssq_x(0)
            hi(0)
            hi(1)
            high_hT(0)
            ssq_x(1)
            hi(2)
            ssq_x(2)
            hi(3)

            def slot_act(s):
                slab, i = divmod(s, 4)
                if s < NT - 1:
                    high_hT(s + 1)
                    if s == 0:
                        ssq_x(NT - 1)
                hi(4 + s)
                if s == 1:
                    act.dma_start(lb[:, :, :], A["lb_raw"]).then_inc(lb_landed, 16)
                    act.dma_start(scan_mask[:, :], A["scan_mask"]).then_inc(lb_landed, 16)
                    act.dma_start(h_norm[:, :], A["hgrn_norm"].partition_broadcast(P)).then_inc(lb_landed, 16)
                    act.dma_start(mask_f[:, :], A["chunk_mask"]).then_inc(lb_landed, 16)
                    act.dma_start(cw[:, :, :], A["conv"]).then_inc(lb_landed, 16)
                    act.dma_start(rel[:, :], A["rel_bias"]).then_inc(rel_landed, 16)
                    act.dma_start(onehot[:, :, :], A["onehot"]).then_inc(rel_landed, 16)
                    act.dma_start(line_add[:, :, :], A["line_add"]).then_inc(rel_landed, 16)
                if s == 3:
                    act.wait_ge(lb_dif, 1)
                    tell(act.activation(lb_b[:, :], lb_a[:, :], ACT.Tanh, scale=0.5), lb_tanh)
                if s == 7:
                    act.wait_ge(line_ready, 3)
                    for a, g in enumerate(GROUPS):
                        keys = A["table_scratch"][a].shape[2]
                        line = lines[:, g, 2 * P - keys:]
                        act.dma_start(A["table_scratch"][a].rearrange("p h j -> h p j"),
                                      bass.AP(line.tensor, line.offset + P - 1, [line.ap[0], [-1, P], [1, keys]])
                                      ).then_inc(line_stored, 16)
                if s == 4 * SL_HQ:
                    act.wait_ge(f_ready, HH)
                    tell(act.activation(HF[:, :, :], HF[:, :, :], ACT.Ln), log_ready)
                h = s - 4 * SL_HQ - 1
                if 0 <= h < HH:
                    if h >= 2:
                        act.wait_ge(prep_done, h - 1)
                    act.wait_ge(G_ready, h + 1)
                    act.activation(E1[:, h % 2, :], HF[:, h, :], ACT.Exp).then_inc(exp_G, 1)
                    act.activation(E2[:, h % 2, :], HF[:, h, :], ACT.Exp, scale=-1.0).then_inc(exp_G, 1)
                    run(act.activation(chunk_decay[:, h, :],
                                       HF[:, h, :].rearrange("p (c j) -> p c j", j=CH)[:, :, CH - 1], ACT.Exp))
                    act.wait_ge(dif_ready, h + 1)
                    tell(act.activation(E3[:, h % 2, :], E3[:, h % 2, :], ACT.Exp), exps_ready)
                for t in range(NT):
                    if s == group_slot(t):
                        act.wait_ge(kdt_done, t + 1)
                        if t:
                            act.wait_ge(kv_done, t)
                        tell(act.activation(kd[:, :, :], quarters(3), ACT.Copy), kd_ready)
                for t in range(NT):
                    if s == group_slot(t) + 3:
                        act.wait_ge(yht_done, t + 1)
                        tell(act.activation(yh_hi[:, :, t * P:(t + 1) * P], quarters(3), ACT.Copy), yh_hi_done)
                    if s == group_slot(t) + 2:
                        act.wait_ge(o_done, HH * (t + 1))
                        if t:
                            act.wait_ge(rstd_ready, NT + t)
                        for h in range(HH):
                            ins = act.activation(junk_h[:, :], quarters(2)[:, h, :], ACT.Square, accum_out=ss[:, h:h + 1])
                            tell(ins, ssq_ready) if h == HH - 1 else run(ins)
                ah = attn_at(s)
                if ah:
                    a, h = ah
                    idx = HEADS * a + h
                    act.wait_ge(max_ready, idx + 1)
                    if idx >= 2:
                        act.wait_ge(pt_done, idx - 1)
                    for n in range(NT):
                        src = scores2[:, n, :] if a == 2 else quarters(2)[:, n, :]
                        dst = PR[:, idx % 2, n, P:]
                        if a == 2 and n == 0:
                            src = scores2[:, n, P:]
                        elif a == 2:
                            dst = PR[:, idx % 2, n, :]
                        ins = act.activation(dst, src, ACT.Exp, bias=stat[:, a, n, h:h + 1],
                                             accum_out=stat[:, a, n, HEADS + h:HEADS + h + 1])
                        tell(ins, exp_done) if n == NT - 1 else run(ins)
                for a in range(2):
                    if s == head_slot(a, HEADS - 1) + 3:
                        act.wait_ge(o_saved, HEADS * (a + 1))
                        for src, dst in ((O[:, :, :], A["O_scratch"][a, :, :]), (stat[:, a, :, :], A["stat_scratch"][a, :, :])):
                            act.dma_start(dst.rearrange("(p n) c -> p n c", n=NT), src).then_inc(O_stored[a], 16)
                    if s == (head_slot(1, HEADS - 1) + 4, head_slot(2, HEADS - 1) + 2)[a]:
                        act.wait_ge(O_stored[a], 32)
                        act.wait_ge(pv_done, 16) if a == 0 else act.wait_ge(pt_done, 24)
                        act.dma_start((On0, On1)[a][:, :, :], A["O_scratch"][a, :, :].rearrange("(t p) c -> p t c", p=P)
                                      ).then_inc(On_landed[a], 16)
                        act.dma_start(stat[:, a, :, :], A["stat_scratch"][a, :, :].rearrange("(t p) c -> p t c", p=P)
                                      ).then_inc(On_landed[a], 16)
                if s == head_slot(0, 0) - 2:
                    act.wait_ge(o_done, HH * NT)
                    act.wait_ge(line_stored, 48)
                    dma_bias(0)
                if s == head_slot(0, 0) - 1:
                    dma_bias(1)
                if s == head_slot(1, HEADS - 1) + 3:
                    act.wait_ge(max_ready, 2 * HEADS)
                    dma_bias(2)
                if s == head_slot(2, HEADS - 1) + 3:
                    act.wait_ge(dif_lse, 1)
                    tell(act.activation(tmp[:, 0:3, :, :], tmp[:, 0:3, :, :], ACT.Exp), exp_lse)
                if s in YA_SLOTS:
                    t = s - YA_SLOTS[0]
                    act.wait_ge(yat_done, t + 1)
                    tell(act.activation(ya_hi[:, :, t * P:(t + 1) * P], quarters(7), ACT.Copy), ya_hi_done)
                act_block(s)

            def dma_bias(a):
                act.dma_start((bias_a, bias_b, bias_c)[a][:, :, :], A["table_scratch"][a]).then_inc(bias_landed[a], 16)

            def act_block(s):
                slab, i = divmod(s, 4)
                src = bank(s % 2)
                act.wait_ge(proj_done, s + 1)
                if slab == SL_HF:
                    tell(act.activation(HF[:, i, :], src, ACT.Tanh, scale=0.5), evac["act"])
                elif slab == SL_HQ:
                    tell(act.activation(HQ[:, i, :], src, ACT.Tanh, scale=0.5), tanh_ready)
                elif slab == SL_OG:
                    if i == 0:
                        act.wait_ge(line_stored, 48)
                    tell(act.activation(HOG[:, i, :], src, ACT.Tanh, scale=0.5), tanh_ready)
                elif slab >= SL_GATE:
                    if slab == SL_GATE + 1 and i == 0:
                        act.wait_ge(yh_split, NT)
                    if slab == SL_GATE + 2 and i == 0:
                        act.wait_ge(scores_done, 3 * HEADS)
                    tell(act.activation(gates[slab - SL_GATE][:, i, :], src, ACT.Tanh, scale=0.5), evac["act"])
                elif slab >= SL_ATT and (slab - SL_ATT) % 3:
                    a, which = divmod(slab - SL_ATT, 3)
                    if a:
                        act.wait_ge(scores_done, HEADS * (a - 1) + (2 * i + 2 if which == 1 else HEADS))
                    elif which == 1:
                        act.wait_ge(prep_done, HH)
                    else:
                        act.wait_ge(o_done, HH * NT)
                    d = STRIDE[GROUPS[a]]
                    dst = (QT if which == 1 else KT)[:, i, :]
                    if d > 1:
                        dst = dst.rearrange("p (r u) -> p r u", r=d)
                        src = src.rearrange("p (u r) -> p r u", r=d)
                    tell(act.activation(dst, src, ACT.Copy), evac["act"])

            for s in range(N_SLOTS):
                slot_act(s)

            act.wait_ge(ya_ready, NT)
            act.dma_start(w_post[:, :], A["post_mix"].partition_broadcast(P)).then_inc(w_post_landed, 16)
            for j in range(KC):
                first = {0: 4, 1: 6, 4: 8, 5: 10, 7: 12}.get(j)
                if first:
                    hi(N_SLOTS + first)
                    hi(N_SLOTS + first + 1)
                act.wait_ge(m_ready, j + 1)
                tell(act.activation(mT[:, 0, j, :], m1[:, :], ACT.Copy, scale=0.5), m_hi)
            hi(PAIRS_UP - 2)
            hi(PAIRS_UP - 1)
            act.wait_ge(br_done, 2 * KC)
            for t in range(NT):
                act.dma_start(x2[:, t, :], A["x"][t * P:(t + 1) * P, :]).then_inc(x2_landed[t], 16)
                if t == 0:
                    act.dma_start(w_pre2[:, :], A["pre_ffn"].partition_broadcast(P)).then_inc(w_pre2_landed, 16)
            hi(PAIRS_UP)

            def split_h2(t):
                act.wait_ge(h2t_done, t + 1)
                tell(act.activation(h2_hi[:, :, t * P:(t + 1) * P],
                                    bank(4 + 2 * (t % 2), 2).rearrange("p b (k c) -> p (b k) c", c=P), ACT.Copy), h2_hi_done)

            for t in range(NT):
                if t:
                    hi(PAIRS_UP + t)
                    split_h2(t - 1)
                act.wait_ge(wo_done, 2 * (t + 1))
                junk = ps[:, 4 + 2 * (t % 2):6 + 2 * (t % 2), :]
                if t >= 2:
                    act.wait_ge(h2_split, t - 1)
                tell(act.activation(junk, ps[:, 2 * (t % 2):2 * (t % 2) + 2, :], ACT.Square, accum_out=ss[:, t:t + 1]), wo_ssq)
                act.wait_ge(wo_res, t + 1)
                tell(act.activation(junk, x2[:, t, :].rearrange("p (b c) -> p b c", b=2), ACT.Square,
                                    accum_out=ss[:, NT + t:NT + t + 1]), wo_ssq)
            hi(PAIRS_UP + 4)
            hi(PAIRS_UP + 5)
            split_h2(NT - 1)
            hi(PAIRS_UP + 6)
            hi(PAIRS_UP + 7)

            def up_tile(f, k, after_first):
                for half in range(2):
                    act.wait_ge(up_done, 2 * f + (half + 1))
                    if after_first:
                        act.wait_ge(conv_done, 2 * f + (half - 1))
                    act.activation(up[half][:, 2:], bank(2 * k + half), ACT.Copy).then_inc(up_copied, 1)
                    act.wait_ge(up_copied, 2 * f + (half + 1))
                    if after_first:
                        act.wait_ge(a_ready, f)
                    c = f + half * FT
                    act.activation(cv[half][:, :], up[half][:, 0:SEQ], ACT.Identity,
                                   scale=cw[:, 0, bass.ds(c, 1)], bias=cw[:, 3, bass.ds(c, 1)]).then_inc(tap0_done, 1)
                act.wait_ge(conv_done, 2 * f + 1)
                act.activation(ge[:, :], cv[0][:, :], ACT.Gelu).then_inc(gelu_done, 1)

            act.wait_ge(pads_ready, 2)
            for k in range(2):
                up_tile(k, k, k > 0)
            first = PAIRS_UP + RING

            def up_four(g):
                for k in range(4):
                    for r in range(2):
                        q = first + 2 * k + r
                        act.wait_ge(raw_landed[q % RAW], 32 * g + 16 * (q // RAW + 1))
                        act.wait_ge(up_done, 8 * g + 4 * (k // 2 + 1))
                        act.activation(ws[:, q % RING, 0, :, :], raw[:, q % RAW, :, :], ACT.Copy).then_inc(hi_done, 1)
                    up_tile(4 * g + (2 + k), k % 2, True)

            def high_a(q):
                act.wait_ge(a_ready, min(q + 1, FT))
                if q >= A_RING:
                    act.wait_ge(down_chunk, q - A_RING + 1)
                act.activation(a_hi[:, q % A_RING, :], aT[:, q % FT, :], ACT.Copy).then_inc(a_hi_done, 1)

            with act.Fori(0, (UPS - 1) // 2 - 1) as g:
                up_four(g)
            for q in range(A_RING):
                high_a(q)
            up_four((UPS - 1) // 2 - 1)

            act.wait_ge(up_done, 4 * UPS)
            act.dma_start(w_ffn[:, :], A["post_ffn"].partition_broadcast(P)).then_inc(wf_landed, 16)
            for q in range(2 * FT):
                if q % 2 == 0 and PAIRS_DOWN + 4 + q // 2 < N_PAIRS:
                    hi(PAIRS_DOWN + 4 + q // 2)
                if q >= A_RING:
                    high_a(q)
                t = q - FT - 2
                if 0 <= t < NT:
                    act.wait_ge(d0_ready, t + 1)
                    act.activation(res[0][:, 0:COLS], bank(4 + t), ACT.Square, accum_out=ss[:, t:t + 1]).then_inc(fin_ssq, 1)
                    act.wait_ge(fin_ssq, t + 1)
            act.wait_ge(a_split, 2 * FT)
            for t in range(NT):
                act.wait_ge(down_tile, t + 1)
                act.activation(junk_d[:, :], bank(t), ACT.Square, accum_out=ss[:, NT + t:NT + t + 1]).then_inc(fin_ssq, 1)
                act.wait_ge(fin_ssq, NT + t + 1)

        @block.vector
        def _(dve):
            run, tell = teller(dve, dve_step)
            roots = [0]

            def root(ssq, width, n, more=EPS, meanwhile=None):
                tell(dve.tensor_scalar(var[:, 0:n], ssq, 1.0 / width, more, ALU.mult, ALU.add), var_ready)
                if meanwhile:
                    meanwhile()
                roots[0] += 1
                dve.wait_ge(rstd_ready, roots[0])

            def norm_x(t):
                dve.wait_ge(ssq_ready, t + 1)
                root(ss[:, t:t + 1], DM, 1)
                if t == 0:
                    dve.wait_ge(w_pre_landed, 16)
                if t >= 2:
                    dve.wait_ge(xt_done, t - 1)
                tell(dve.scalar_tensor_tensor(xn[:, t % 2, :], x_in[:, t, :], rstd[:, 0:1], w_pre[:, :],
                                              ALU.mult, ALU.mult), xn_ready)

            norm_x(0)
            dve.wait_ge(hT_hi, 1)
            low_hT(0, tell)
            norm_x(1)

            def slot_dve(s):
                slab, i = divmod(s, 4)
                if s < NT - 1:
                    if s < NT - 2:
                        norm_x(s + 2)
                    dve.wait_ge(hT_hi, s + 2)
                    low_hT(s + 1, tell)
                if s == 3:
                    dve.wait_ge(lb_landed, 80)
                    run(dve.tensor_copy(chunk_mask[:, :], mask_f[:, :]))
                    tell(dve.tensor_tensor(lb_a[:, :], lb[:, 0, :], lb[:, 1, :], ALU.subtract), lb_dif)
                    dve.wait_ge(lb_tanh, 1)
                    run(dve.tensor_scalar(lb_a[:, :], lb_b[:, :], -0.25, 0.25, ALU.mult, ALU.add))
                    run(dve.tensor_scalar(lb_b[:, :], lb_b[:, :], 0.25, 0.75, ALU.mult, ALU.add))
                    dve.wait_ge(rel_landed, 48)
                if 4 <= s < 7:
                    dve.wait_ge(line_done, s - 3)
                    tell(dve.tensor_tensor(lines[:, s - 4, :], ps[0:HEADS, 6 + s % 2, 0:LINE], line_add[:, s - 4, :],
                                           ALU.add), line_ready)
                h = s - 4 * SL_HQ
                if 0 <= h < HH:
                    if h == 0:
                        dve.wait_ge(log_ready, 1)
                    tell(dve.tensor_tensor_scan(HF[:, h, :], scan_mask[:, :], HF[:, h, :], 0.0, ALU.mult, ALU.add), G_ready)
                    G = HF[:, h, :].rearrange("p (c j) -> p c j", j=CH)
                    tell(dve.tensor_tensor(E3[:, h % 2, :].rearrange("p (c j) -> p c j", j=CH),
                                           G[:, :, CH - 1:CH].to_broadcast([P, SEQ // CH, CH]), G, ALU.subtract), dif_ready)
                h -= 1
                if 0 <= h < HH:
                    dve.wait_ge(exp_G, 2 * h + 2)
                    run(dve.scalar_tensor_tensor(HQ[:, h, :], HQ[:, h, :], 0.5, E1[:, h % 2, :], ALU.mult, ALU.mult))
                    run(dve.tensor_tensor(HKX[:, h, :], HK[:, h, :], E2[:, h % 2, :], ALU.mult))
                    dve.wait_ge(exps_ready, h + 1)
                    tell(dve.tensor_tensor(HK[:, h, :], HK[:, h, :], E3[:, h % 2, :], ALU.mult), prep_done)
                for t in range(NT):
                    if s == group_slot(t):
                        if t == 0:
                            run(dve.memset(carry[:, 0, :, :], 0.0))
                            run(dve.memset(AT[:, :, :], 0.0))
                        else:
                            dve.wait_ge(o_done, HH * t)
                        dve.wait_ge(at_done, t + 1)
                        tell(dve.copy_predicated(AT[:, :, :], chunk_mask[:, :].unsqueeze(1).to_broadcast([P, HH, P]),
                                                 quarters(2)), at_ready)
                        dve.wait_ge(kv_done, t + 1)
                        for h in range(HH):
                            for c in range(4):
                                old = carry[:, t % 2, h, :] if c == 0 else states[:, h, c - 1, :]
                                new = carry[:, (t + 1) % 2, h, :] if c == 3 else states[:, h, c, :]
                                ins = dve.scalar_tensor_tensor(new, old, chunk_decay[:, h, 4 * t + c:4 * t + c + 1],
                                                               quarters(4 + c)[:, h, :], ALU.mult, ALU.add)
                                tell(ins, chain_done) if c == 3 else run(ins)
                for t in range(NT):
                    if s == group_slot(t) + 3:
                        dve.wait_ge(yh_hi_done, t + 1)
                        tell(dve.tensor_tensor(yh_lo[:, :, t * P:(t + 1) * P], quarters(3),
                                               yh_hi[:, :, t * P:(t + 1) * P].bitcast(F32), ALU.subtract), yh_split)
                    if s == group_slot(t) + 2:
                        dve.wait_ge(ssq_ready, NT + t + 1)
                        root(ss[:, 0:HH], P, HH)
                        if t:
                            dve.wait_ge(yht_done, t)
                        tell(dve.tensor_tensor(yo[:, :, :], quarters(2), rstd[:, 0:HH].unsqueeze(2).to_broadcast([P, HH, P]),
                                               ALU.mult), o_read)
                        run(dve.tensor_tensor(yo[:, :, :], yo[:, :, :], h_norm[:, :].unsqueeze(1).to_broadcast([P, HH, P]),
                                              ALU.mult))
                        tell(dve.scalar_tensor_tensor(yo[:, :, :].rearrange("p h c -> p (h c)"),
                                                      yo[:, :, :].rearrange("p h c -> p (h c)"), 0.5, HOG[:, t, :],
                                                      ALU.mult, ALU.mult), yo_ready)
                if s >= 2 and attn_at(s - 2):
                    a, h = attn_at(s - 2)
                    dve.wait_ge(pv_done, HEADS * a + h + 1)
                    if a and h == 0:
                        dve.wait_ge(O_stored[a - 1], 32)
                    tell(dve.tensor_copy(O[:, :, h * HD:(h + 1) * HD],
                                         ps[:, 6, 0:NT * HD].rearrange("p (n d) -> p n d", n=NT)), o_saved)
                if attn_at(s):
                    a, h = attn_at(s)
                    if h == 0:
                        dve.wait_ge(bias_landed[a], 16)
                    dve.wait_ge(scores_done, HEADS * a + h + 1)
                    if a == 2:
                        run(dve.scalar_tensor_tensor(scores2[:, 0, P:], scores2[:, 0, P:], HD ** -0.5, bias_c[:, h, P:],
                                                     ALU.mult, ALU.add))
                        run(dve.scalar_tensor_tensor(scores2[:, 1:, :], scores2[:, 1:, :], HD ** -0.5,
                                                     bias_c[:, h, :].unsqueeze(1).to_broadcast([P, NT - 1, 2 * P]),
                                                     ALU.mult, ALU.add))
                        run(dve.tensor_reduce(mx[:, 0:1], scores2[:, 0, P:], AX_X, ALU.max))
                        run(dve.tensor_reduce(mx[:, 1:], scores2[:, 1:, :], AX_X, ALU.max))
                    else:
                        table = (bias_a, bias_b)[a]
                        run(dve.scalar_tensor_tensor(quarters(2), quarters(2), HD ** -0.5,
                                                     table[:, h, :].unsqueeze(1).to_broadcast([P, NT, P]),
                                                     ALU.mult, ALU.add))
                        run(dve.tensor_reduce(mx[:, :], quarters(2), AX_X, ALU.max))
                    tell(dve.tensor_scalar(stat[:, a, :, h], mx[:, :], -1.0, None, ALU.mult), max_ready)
                if s >= 1 and attn_at(s - 1):
                    a, h = attn_at(s - 1)
                    idx = HEADS * a + h
                    dve.wait_ge(pt_done, idx + 1)
                    if idx:
                        dve.wait_ge(pv_done, idx)
                    k = 7 if a == 2 else 4
                    tell(dve.tensor_copy(PT[:, 0:k, :], pt_banks[:, 0:k, :]), pt_ready)
                if s == head_slot(2, HEADS - 1) + 3:
                    dve.wait_ge(On_landed[0], 32)
                    dve.wait_ge(On_landed[1], 32)
                    low, lse = [stat[:, a, :, 0:HEADS] for a in range(3)], [stat[:, a, :, HEADS:] for a in range(3)]
                    run(dve.tensor_tensor(tmp[:, 3, :, :], low[0], low[1], ALU.min))
                    run(dve.tensor_tensor(tmp[:, 3, :, :], tmp[:, 3, :, :], low[2], ALU.min))
                    for a in range(3):
                        ins = dve.tensor_tensor(tmp[:, a, :, :], tmp[:, 3, :, :], low[a], ALU.subtract)
                        tell(ins, dif_lse) if a == 2 else run(ins)
                    dve.wait_ge(exp_lse, 1)
                    for a in range(3):
                        run(dve.tensor_tensor(low[a], tmp[:, a, :, :], lse[a], ALU.mult))
                    run(dve.tensor_tensor(tmp[:, 3, :, :], low[0], low[1], ALU.add))
                    run(dve.tensor_tensor(tmp[:, 3, :, :], tmp[:, 3, :, :], low[2], ALU.add))
                    run(dve.reciprocal(tmp[:, 3, :, :], tmp[:, 3, :, :]))
                    for a in range(3):
                        run(dve.tensor_tensor(tmp[:, a, :, :], tmp[:, a, :, :], tmp[:, 3, :, :], ALU.mult))
                if s + 1 in YA_SLOTS:
                    t = s + 1 - YA_SLOTS[0]
                    parts = [x[:, t, :].rearrange("p (h d) -> p h d", h=HEADS) for x in (On0, On1, O)]
                    for a in range(3):
                        run(dve.tensor_tensor(parts[a], parts[a], tmp[:, a, t, :].unsqueeze(2).to_broadcast([P, HEADS, HD]),
                                              ALU.mult))
                    run(dve.tensor_tensor(O[:, t, :], O[:, t, :], On0[:, t, :], ALU.add))
                    tell(dve.tensor_tensor(O[:, t, :], O[:, t, :], On1[:, t, :], ALU.add), ya_ready)
                if s in YA_SLOTS:
                    t = s - YA_SLOTS[0]
                    dve.wait_ge(ya_hi_done, t + 1)
                    tell(dve.tensor_tensor(ya_lo[:, :, t * P:(t + 1) * P], quarters(7),
                                           ya_hi[:, :, t * P:(t + 1) * P].bitcast(F32), ALU.subtract), ya_split)
                dve_block(s)

            def dve_block(s):
                slab, i = divmod(s, 4)
                src = bank(s % 2)
                if slab == SL_HF:
                    dve.wait_ge(evac["act"], i + 1)
                    run(dve.tensor_scalar(E3[:, 0, :], HF[:, i, :], lb_a[:, i:i + 1], lb_b[:, i:i + 1], ALU.mult, ALU.add))
                    run(dve.tensor_scalar(HK[:, i, :], HF[:, i, :], -1.0, 1.0, ALU.mult, ALU.add))
                    run(dve.tensor_scalar(HK[:, i, :], HK[:, i, :], lb_a[:, i:i + 1], None, ALU.mult))
                    tell(dve.tensor_copy(HF[:, i, :], E3[:, 0, :]), f_ready)
                elif slab == SL_HQ or slab == SL_OG:
                    dve.wait_ge(tanh_ready, i + (1 if slab == SL_HQ else 5))
                    dst = (HQ if slab == SL_HQ else HOG)[:, i, :]
                    tell(dve.scalar_tensor_tensor(dst, dst, 1.0, src, ALU.add, ALU.mult), evac["dve"])
                elif slab == SL_HI:
                    dve.wait_ge(proj_done, s + 1)
                    tell(dve.tensor_copy(HV[:, i, :], src), evac["dve"])
                elif evacuator(s) == "dve":
                    a = (slab - SL_ATT) // 3
                    dve.wait_ge(proj_done, s + 1)
                    tell(dve.tensor_copy((VA, VB, VA)[a][:, i, :], src), evac["dve"])

            for s in range(N_SLOTS):
                slot_dve(s)

            for j in range(KC):
                b = 2 + 2 * (j % 2)
                half, i = divmod(j, 4)
                dve.wait_ge(br_done, 2 * j + 1)
                run(dve.scalar_tensor_tensor(m1[:, :], gates[2 * half][:, i, :], 1.0, bank(b), ALU.add, ALU.mult))
                dve.wait_ge(br_done, 2 * j + 2)
                tell(dve.scalar_tensor_tensor(m2[:, :], gates[2 * half + 1][:, i, :], 1.0, bank(b + 1), ALU.add, ALU.mult),
                     br_read)
                tell(dve.tensor_tensor(m1[:, :], m1[:, :], m2[:, :], ALU.add), m_ready)
                dve.wait_ge(m_hi, j + 1)
                tell(dve.scalar_tensor_tensor(mT[:, 1, j, :], m1[:, :], 0.5, mT[:, 0, j, :].bitcast(F32),
                                              ALU.mult, ALU.subtract), m_split)

            def low_h2(t):
                dve.wait_ge(h2_hi_done, t + 1)
                cols = slice(t * P, (t + 1) * P)
                tell(dve.tensor_tensor(h2_lo[:, :, cols], bank(4 + 2 * (t % 2), 2).rearrange("p b (k c) -> p (b k) c", c=P),
                                       h2_hi[:, :, cols].bitcast(F32), ALU.subtract), h2_split)

            dve.wait_ge(w_post_landed, 16)
            for t in range(NT):
                b = 2 * (t % 2)
                if t:
                    low_h2(t - 1)
                dve.wait_ge(wo_ssq, 2 * t + 1)
                root(ss[:, t:t + 1], DM, 1)
                tell(dve.scalar_tensor_tensor(mixed[:, :], ps[:, b:b + 2, :].rearrange("p b c -> p (b c)"), rstd[:, 0:1],
                                              w_post[:, :], ALU.mult, ALU.mult), wo_read)
                dve.wait_ge(x2_landed[t], 16)
                tell(dve.tensor_tensor(x2[:, t, :], x2[:, t, :], mixed[:, :], ALU.add), wo_res)
                dve.wait_ge(wo_ssq, 2 * t + 2)
                root(ss[:, NT + t:NT + t + 1], DM, 1)
                if t == 0:
                    dve.wait_ge(w_pre2_landed, 16)
                tell(dve.scalar_tensor_tensor(mixed[:, :], x2[:, t, :], rstd[:, 0:1], w_pre2[:, :], ALU.mult, ALU.mult),
                     xn2_ready)
            tell(dve.memset(up[0][:, 0:2], 0.0), pads_ready)
            tell(dve.memset(up[1][:, 0:2], 0.0), pads_ready)
            low_h2(NT - 1)


            def up_tile(f):
                for half in range(2):
                    c = f + half * FT
                    dve.wait_ge(tap0_done, 2 * f + (half + 1))
                    dve.scalar_tensor_tensor(cv[half][:, :], up[half][:, 1:SEQ + 1], cw[:, 1, bass.ds(c, 1)], cv[half][:, :],
                                             ALU.mult, ALU.add).then_inc(tap1_done, 1)
                    dve.wait_ge(tap1_done, 2 * f + (half + 1))
                    dve.scalar_tensor_tensor(cv[half][:, :], up[half][:, 2:], cw[:, 2, bass.ds(c, 1)], cv[half][:, :],
                                             ALU.mult, ALU.add).then_inc(conv_done, 1)
                dve.wait_ge(conv_done, 2 * f + 2)
                dve.wait_ge(gelu_done, f + 1)
                dve.tensor_tensor(aT[:, bass.ds(f, 1), :].rearrange("p o c -> p (o c)"), ge[:, :], cv[1][:, :],
                                  ALU.mult).then_inc(a_ready, 1)

            for k in range(2):
                up_tile(k)
            def low_a(q):
                dve.wait_ge(a_hi_done, q + 1)
                dve.tensor_tensor(a_lo[:, q % A_RING, :], aT[:, q % FT, :], a_hi[:, q % A_RING, :].bitcast(F32),
                                  ALU.subtract).then_inc(a_split, 1)

            def up_four(g):
                for k in range(4):
                    up_tile(4 * g + (2 + k))

            with dve.Fori(0, (UPS - 1) // 2 - 1) as g:
                up_four(g)
            for q in range(A_RING):
                low_a(q)
            up_four((UPS - 1) // 2 - 1)

            for q in range(A_RING, 2 * FT):
                low_a(q)
                t = q - FT - 1
                if 0 <= t < NT:
                    dve.wait_ge(down_chunk, FT)
                    dve.wait_ge(wf_landed, 16)
                    tell(dve.tensor_tensor(d0[:, t, :], bank(4 + t), w_ffn[:, 0:COLS], ALU.mult), d0_ready)
            dve.wait_ge(a_split, 2 * FT)
            dve.wait_ge(fin_ssq, NT)
            run(dve.tensor_scalar(var0[:, :], ss[:, 0:NT], 1.0 / DM, EPS, ALU.mult, ALU.add))
            for t in range(NT):
                if t >= 2:
                    dve.wait_ge(out_stored[t % 2], 32)
                r = res[t % 2]
                dve.wait_ge(fin_ssq, NT + t + 1)
                root(ss[:, NT + t:NT + t + 1], DM, 1, more=var0[:, t:t + 1], meanwhile=lambda: run(
                    dve.tensor_tensor(r[:, COLS:], bank(t), w_ffn[:, COLS:], ALU.mult)))
                tell(dve.scalar_tensor_tensor(r[:, 0:COLS], d0[:, t, :], rstd[:, 0:1], x2[:, t, 0:COLS], ALU.mult, ALU.add),
                     out_ready)
                tell(dve.scalar_tensor_tensor(r[:, COLS:], r[:, COLS:], rstd[:, 0:1], x2[:, t, COLS:], ALU.mult, ALU.add),
                     out_ready)

        @block.tensor
        def _(pe):
            def three(dst, pairs, after=None):
                last = len(pairs) - 1
                for n, (w, m) in enumerate(pairs):
                    for step in (after or {}).get(n, ()):
                        step()
                    pe.matmul(dst, w[0], m[0], start=n == 0, stop=False)
                    pe.matmul(dst, w[0], m[1], start=False, stop=False)
                    ins = pe.matmul(dst, w[1], m[0], start=False, stop=n == last)
                return ins

            def w_cols(n0, k, c0=0, width=COLS):
                w = split_place(n0 + k // 2)
                return tuple(ws[:, w, part, k % 2, c0:c0 + width] for part in range(2))

            def tokens(k, t, d):
                out = []
                for part in range(2):
                    row = hT[:, part, k, :]
                    out.append(row[:, t * P:(t + 1) * P] if d == 1 else row.rearrange("p (u r) -> p r u", r=d)[:, t, :])
                return tuple(out)

            def project(s, middle):
                slab, i = divmod(s, 4)
                if s >= 2:
                    pe.wait_ge(evac[evacuator(s - 2)], evacuated(s - 2))
                by_token = slab in (SL_HI, SL_OG) or (SL_ATT <= slab < SL_GATE and (slab - SL_ATT) % 3 == 0)
                if by_token:
                    d = STRIDE[GROUPS[(slab - SL_ATT) // 3]] if slab >= SL_ATT else 1
                    pairs = [(tokens(k, i, d), w_cols(4 * slab, k)) for k in range(KC)]
                else:
                    pairs = [(w_cols(4 * slab, k, i * P, P), (hT[:, 0, k, :], hT[:, 1, k, :])) for k in range(KC)]
                after = {KC // 2 if s else 2: [middle]}
                for t in range(NT):
                    if s == group_slot(t):
                        for h in range(HH):
                            after.setdefault(3 + h, []).append(lambda t=t, h=h: recur_kv(t, h))
                if i == 0:
                    for r in range(4):
                        after.setdefault(2 * r, []).append(lambda r=r: pe.wait_ge(lo_done, 4 * slab + r + 1))
                three(bank(s % 2), pairs, after).then_inc(proj_done, 1)

            def transpose_x(t):
                pe.wait_ge(xn_ready, t + 1)
                if t >= 2:
                    pe.wait_ge(hT_ready, t - 1)
                for k in range(KC):
                    ins = pe.transpose(quarters(2 + 2 * (t % 2) + k // 4)[:, k % 4, :], xn[:, t % 2, k * P:(k + 1) * P],
                                       ident[:, :])
                ins.then_inc(xt_done, 1)

            pe.wait_ge(ident_landed, 16)
            transpose_x(0)

            def scores(a, h):
                idx = HEADS * a + h
                r = slice(HD * (h % 2), HD * (h % 2) + HD)
                j = h // 2
                if idx == 0:
                    pe.wait_ge(o_read, NT)
                    pe.wait_ge(yh_split, NT)
                else:
                    pe.wait_ge(exp_done, idx)
                if h % 2 == 0:
                    pe.wait_ge(evac["act"], evacuated(4 * (SL_ATT + 3 * a + 2) + j))
                for n in range(NT):
                    q = QT[r, j, n * P:(n + 1) * P]
                    if a < 2:
                        ins = pe.matmul(quarters(2)[:, n, :], q, KT[r, j, n * P:(n + 1) * P], start=True, stop=True)
                    elif n == 0:
                        ins = pe.matmul(scores2[:, 0, P:], q, KT[r, j, 0:P], start=True, stop=True)
                    else:
                        ins = pe.matmul(scores2[:, n, :], q, KT[r, j, (n - 1) * P:(n + 1) * P], start=True, stop=True)
                ins.then_inc(scores_done, 1)

            def transpose_probs(a, h):
                idx = HEADS * a + h
                pe.wait_ge(exp_done, idx + 1)
                if idx:
                    pe.wait_ge(pt_ready, idx)
                else:
                    pe.wait_ge(chain_done, HH * NT)
                for n in range(NT):
                    ins = pe.transpose(pt_banks[:, n, :], PR[:, idx % 2, n, P:], ident[:, :])
                if a == 2:
                    for n in range(1, NT):
                        ins = pe.transpose(pt_banks[:, 3 + n, :], PR[:, idx % 2, n, 0:P], ident[:, :])
                ins.then_inc(pt_done, 1)

            def weigh_values(a, h):
                idx = HEADS * a + h
                pe.wait_ge(pt_ready, idx + 1)
                if idx:
                    pe.wait_ge(o_saved, idx)
                V = (VA, VB, VA)[a]
                cols = slice(h * HD, (h + 1) * HD)
                for n in range(NT):
                    dst = ps[:, 6, n * HD:(n + 1) * HD]
                    if a == 2 and n:
                        pe.matmul(dst, PT[:, 3 + n, :], V[:, n - 1, cols], start=True, stop=False)
                    ins = pe.matmul(dst, PT[:, n, :], V[:, n, cols], start=not (a == 2 and n), stop=True)
                ins.then_inc(pv_done, 1)

            def recur_first(t):
                cols = slice(t * P, (t + 1) * P)
                if t == 0:
                    pe.wait_ge(prep_done, HH)
                    pe.wait_ge(evac["dve"], 4)
                else:
                    pe.wait_ge(o_read, t)
                for h in range(HH):
                    ins = pe.matmul(quarters(2)[:, h, :], HKX[:, h, cols], HQ[:, h, cols], start=True, stop=True)
                ins.then_inc(at_done, 1)
                if t >= 2:
                    pe.wait_ge(yh_split, t - 1)
                for h in range(HH):
                    ins = pe.transpose(quarters(3)[:, h, :], HK[:, h, cols], ident[:, :])
                ins.then_inc(kdt_done, 1)

            def recur_kv(t, h):
                pe.wait_ge(kd_ready, t + 1)
                if t:
                    pe.wait_ge(chain_done, HH * t)
                for c in range(4):
                    rows = slice(CH * c, CH * (c + 1))
                    ins = pe.matmul(quarters(4 + c)[:, h, :], kd[rows, h, :], HV[rows, t, h * P:(h + 1) * P],
                                    start=True, stop=True)
                if h == HH - 1:
                    ins.then_inc(kv_done, 1)

            def recur_out(t, h):
                pe.wait_ge(at_ready, t + 1)
                pe.wait_ge(chain_done, HH * t + h + 1)
                pe.matmul(quarters(2)[:, h, :], AT[:, h, :], HV[:, t, h * P:(h + 1) * P], start=True, stop=False,
                          skip_group_check=True)
                for c in range(4):
                    state = carry[:, t % 2, h, :] if c == 0 else states[:, h, c - 1, :]
                    q = HQ[:, h, t * P + CH * c:t * P + CH * (c + 1)]
                    ins = pe.matmul(quarters(2)[CH * c:CH * (c + 1), h, :], q, state, start=False, stop=True,
                                    skip_group_check=True)
                ins.then_inc(o_done, 1)

            for s in range(N_SLOTS):
                if s < NT:
                    pe.wait_ge(hT_ready, s + 1)
                if attn_at(s):
                    scores(*attn_at(s))
                for t in range(NT):
                    if s == group_slot(t):
                        recur_first(t)
                    if s == group_slot(t) + 2:
                        recur_out(t, 2)
                        recur_out(t, 3)

                def middle(s=s):
                    if s >= 1 and attn_at(s - 1):
                        transpose_probs(*attn_at(s - 1))
                    for t in range(NT):
                        if s == group_slot(t) + 1:
                            recur_out(t, 0)
                            recur_out(t, 1)
                    for t in range(NT):
                        if s == group_slot(t) + 3:
                            pe.wait_ge(yo_ready, t + 1)
                            if t + 1 < NT:
                                pe.wait_ge(kd_ready, t + 2)
                            for h in range(HH):
                                ins = pe.transpose(quarters(3)[:, h, :], yo[:, h, :], ident[:, :])
                            ins.then_inc(yht_done, 1)
                    if s < NT - 1:
                        transpose_x(s + 1)
                    if 4 <= s < 7:
                        pe.wait_ge(rel_landed, 48)
                        if s == 6:
                            pe.wait_ge(line_ready, 1)
                        pe.matmul(ps[0:HEADS, 6 + s % 2, 0:LINE], rel[:, (s - 4) * HEADS:(s - 3) * HEADS],
                                  onehot[:, s - 4, :], start=True, stop=True).then_inc(line_done, 1)
                    if s in YA_SLOTS:
                        t = s - YA_SLOTS[0]
                        pe.wait_ge(ya_ready, t + 1)
                        if t:
                            pe.wait_ge(ya_split, t)
                        for c in range(4):
                            ins = pe.transpose(quarters(7)[:, c, :], O[:, t, c * P:(c + 1) * P], ident[:, :])
                        ins.then_inc(yat_done, 1)

                project(s, middle)
                if s >= 1 and attn_at(s - 1):
                    weigh_values(*attn_at(s - 1))

            pe.wait_ge(ya_split, NT)
            for j in range(KC):
                half, i = divmod(j, 4)
                slab = SL_BR + half
                if j >= 2:
                    pe.wait_ge(br_read, j - 1)
                for part, y in enumerate(((ya_hi, ya_lo), (yh_hi, yh_lo))):
                    after = {}
                    if i == 0:
                        after = {2 * r: [lambda r=r: pe.wait_ge(lo_done, 4 * slab + 2 * part + r + 1)] for r in range(2)}
                    three(bank(2 + 2 * (j % 2) + part),
                          [(w_cols(4 * slab, 4 * part + k, i * P, P), (y[0][:, k, :], y[1][:, k, :])) for k in range(4)],
                          after).then_inc(br_done, 1)

            def transpose_h2(t):
                pe.wait_ge(xn2_ready, t + 1)
                if t >= 2:
                    pe.wait_ge(h2_split, t - 1)
                for k in range(KC):
                    ins = pe.transpose(quarters(4 + 2 * (t % 2) + k // 4)[:, k % 4, :], mixed[:, k * P:(k + 1) * P], ident[:, :])
                ins.then_inc(h2t_done, 1)

            pe.wait_ge(evac["act"], evacuated(N_SLOTS - 1))
            for t in range(NT):
                if t >= 2:
                    pe.wait_ge(wo_read, t - 1)
                for half in range(2):
                    slab = SL_WO + half
                    after = {}
                    if t == 0:
                        for k in range(KC):
                            after[k] = [lambda k=k: pe.wait_ge(lo_done, 4 * slab + k // 2 + 1)]
                            if half == 0:
                                after[k].append(lambda k=k: pe.wait_ge(m_split, k + 1))
                    elif half == 1:
                        after[KC - 2] = [lambda: transpose_h2(t - 1)]
                    three(bank(2 * (t % 2) + half),
                          [(tuple(mT[:, part, k, t * P:(t + 1) * P] for part in range(2)), w_cols(4 * slab, k))
                           for k in range(KC)], after).then_inc(wo_done, 1)

            def up_block(k, half, place0, tokens=slice(0, SEQ), after=None):
                pairs = []
                for c in range(KC):
                    cols = slice(256 * half + k * P, 256 * half + (k + 1) * P)
                    w = place0 + c // 2
                    pairs.append(((ws[:, w, 0, c % 2, cols], ws[:, w, 1, c % 2, cols]),
                                  (h2_hi[:, c, tokens], h2_lo[:, c, tokens])))
                return three(ps[:, 2 * k + half, tokens], pairs, after)

            pe.wait_ge(h2_split, NT // 2)
            pe.wait_ge(lo_done, PAIRS_UP + 4)
            for k in range(2):
                pe.wait_ge(wo_read, NT - 1 + k)
                for half in range(2):
                    last = k == 1 and half == 1
                    up_block(k, half, UP0_PLACE, slice(0, SEQ // 2), {KC // 2 - 1: [lambda: transpose_h2(NT - 1)]} if last else None)
            pe.wait_ge(h2_split, NT)
            for k in range(2):
                for half in range(2):
                    up_block(k, half, UP0_PLACE, slice(SEQ // 2, SEQ)).then_inc(up_done, 1)
            with pe.Fori(0, (UPS - 1) // 2) as g:
                for u in range(2):
                    pe.wait_ge(lo_done, 8 * g + (PAIRS_UP + 4 * (u + 2)))
                    for k in range(2):
                        for half in range(2):
                            pe.wait_ge(up_copied, 8 * g + (4 * u + 2 * k + half + 1))
                            up_block(k, half, split_place(PAIRS_UP + 4 * (u + 1))).then_inc(up_done, 1)

            def down(half, q, t):
                w, k = split_place(PAIRS_DOWN + q // 2), q % FT
                a0, a1 = (x[:, q % A_RING, t * P:(t + 1) * P] for x in (a_hi, a_lo))
                w0, w1 = ws[:, w, 0, q % 2, :], ws[:, w, 1, q % 2, :]
                dst = bank(4 * (1 - half) + t)
                pe.matmul(dst, a0, w0, start=k == 0, stop=False)
                pe.matmul(dst, a0, w1, start=False, stop=False)
                return pe.matmul(dst, a1, w0, start=False, stop=k == FT - 1)

            for q in range(2 * FT - 4):
                half = q // FT
                if q == FT:
                    pe.wait_ge(up_copied, 2 * FT)
                pe.wait_ge(a_split, q + 1)
                pe.wait_ge(lo_done, PAIRS_DOWN + q // 2 + 1)
                for t in range(NT):
                    ins = down(half, q, t)
                ins.then_inc(down_chunk, 1)
            pe.wait_ge(a_split, 2 * FT)
            pe.wait_ge(lo_done, N_PAIRS)
            for t in range(NT):
                for q in range(2 * FT - 4, 2 * FT):
                    ins = down(1, q, t)
                ins.then_inc(down_tile, 1)


def bucket(dist):
    n = np.maximum(dist, 0)
    nf = np.maximum(n, 1).astype(np.float32)
    large = 16 + (np.log(nf / np.float32(16)) / np.float32(math.log(2048 / 16)) * np.float32(16)).astype(np.int32)
    return np.where(n < 16, n, np.minimum(large, 31))


def constants():
    x = np.arange(LINE)
    dist = 2 * P - 1 - x
    ok = (dist >= 0) & (dist <= P)
    onehot = np.zeros((32, 3, LINE), np.float32)
    line_add = np.full((HEADS, 3, LINE), NEG, np.float32)
    for g, (d, stride) in enumerate(zip(DILATION, STRIDE)):
        b = bucket(dist * stride)
        use = ok & (dist % (d // stride) == 0)
        onehot[b[use], g, x[use]] = 1.0
        line_add[:, g, use] = 0.0
    j, i = np.arange(P)[:, None], np.arange(P)[None, :]
    return {
        "onehot": onehot,
        "line_add": line_add,
        "ident": np.eye(P, dtype=np.float32),
        "chunk_mask": ((j // CH == i // CH) & (j <= i)).astype(np.float32),
        "scan_mask": np.broadcast_to((np.arange(SEQ) % CH != 0).astype(np.float32), (P, SEQ)),
    }


def stream(w_in, w_branch_attn, w_branch_hgrn, w_out, w_up, w_down):
    attn, hg, gate = 4608, 4608, 4608 + 2048
    qkv = lambda g, which: w_in[:, (3 * g + which) * COLS:(3 * g + which + 1) * COLS]
    hcol = lambda n: w_in[:, hg + n * COLS:hg + (n + 1) * COLS]
    slabs = [hcol(2), hcol(1), hcol(0), hcol(3)]
    for g in GROUPS:
        slabs += [qkv(g, 2), qkv(g, 0), qkv(g, 1)]
    for half in range(2):
        for b in range(2):
            at = gate + b * DM + half * COLS
            slabs.append(w_in[:, at:at + COLS])
    for half in range(2):
        c = slice(half * COLS, (half + 1) * COLS)
        slabs.append(np.concatenate([w_branch_attn[:, c], w_branch_hgrn[:, c]], 0))
    for half in range(2):
        slabs.append(w_out[:, half * COLS:(half + 1) * COLS])
    for u in range(UPS):
        slabs.append(np.concatenate([w_up[:, 256 * u:256 * (u + 1)], w_up[:, DFF + 256 * u:DFF + 256 * (u + 1)]], 1))
    rows = np.concatenate(slabs + [w_down[:, 0:COLS], w_down[:, COLS:]], 0)
    return np.ascontiguousarray(rows.reshape(N_PAIRS, 2, P, COLS).transpose(0, 2, 1, 3))


def kernel(x, pre_mix_norm, w_in, rel_bias, hgrn_lb_raw, hgrn_norm, w_branch_attn, w_branch_hgrn, w_out,
           post_mix_norm, pre_ffn_norm, w_up, conv_w, conv_b, w_down, post_ffn_norm):
    import concourse.bacc as bacc
    from concourse.bass_utils import run_bass_kernel_spmd

    arrays = {
        "x": x[0],
        "stream": stream(*(np.asarray(w)[0] for w in (w_in, w_branch_attn, w_branch_hgrn, w_out, w_up, w_down))),
        "pre_mix": pre_mix_norm[0], "post_mix": post_mix_norm[0], "pre_ffn": pre_ffn_norm[0], "post_ffn": post_ffn_norm[0],
        "rel_bias": rel_bias,
        "lb_raw": np.asarray(hgrn_lb_raw).reshape(2, HH, P).transpose(2, 0, 1),
        "hgrn_norm": hgrn_norm[0],
        "conv": np.concatenate([conv_w[0], conv_b], 0).reshape(4, 2 * FT, P).transpose(2, 0, 1),
        **constants(),
    }
    nc = bacc.Bacc("TRN2", target_bir_lowering=False, num_devices=1)
    fed, A = {}, {}
    for name, a in arrays.items():
        a = np.ascontiguousarray(a)
        fed[f"in_{name}"] = a
        A[name] = nc.dram_tensor(f"in_{name}", a.shape, mybir.dt.from_np(a.dtype), kind="ExternalInput").ap()
    A["table_scratch"] = [nc.dram_tensor(f"table_scratch{a}", (P, HEADS, P if a < 2 else 2 * P), F32, kind="Internal").ap()
                          for a in range(3)]
    for name, shape in (("O_scratch", (2, SEQ, COLS)), ("stat_scratch", (2, SEQ, 2 * HEADS))):
        A[name] = nc.dram_tensor(name, shape, F32, kind="Internal").ap()
    A["out"] = nc.dram_tensor("out", (SEQ, DM), F32, kind="ExternalOutput").ap()
    build(nc, A)
    got = run_bass_kernel_spmd(nc, [fed], core_ids=[0]).results[0]["out"]
    return got.reshape(1, SEQ, DM)
```
